# Optimizing a Trainium2 kernel written in Bass

```python
import math
import jax
import jax.numpy as jnp
from jax import lax
import numpy as np

D_MODEL = 1024
BATCH = 1
SEQ = 1024
DEPTH = 1
DEC_BATCH = 8
DEC_SEQ = 8
PAST_LEN = 1024
PAGE_SIZE = 128

N_HEADS = 16
HEAD_DIM = 64
N_KV_HEADS = 4
GQA_GROUP = N_HEADS // N_KV_HEADS
WINDOW = 128
ATTN_BLOCK = WINDOW
Q_DIM = N_HEADS * HEAD_DIM
KV_DIM = N_KV_HEADS * HEAD_DIM
N_BUCKETS = 32
MAX_EXACT = N_BUCKETS // 2
MAX_DISTANCE = 128
D_CONV = D_MODEL
CONV_WIDTH = 31
N_GROUPS = 4
EXPERTS_PER_GROUP = 8
N_EXPERTS = N_GROUPS * EXPERTS_PER_GROUP
TOP_K = 2
D_EXPERT = 256
MOE_BLOCK = 128
EPS = 1e-6
IN_DIM = 2 * D_CONV + Q_DIM + 2 * KV_DIM + 2 * D_MODEL
SPLITS = [D_CONV, 2 * D_CONV, 2 * D_CONV + Q_DIM, 2 * D_CONV + Q_DIM + KV_DIM,
          2 * D_CONV + Q_DIM + 2 * KV_DIM, 2 * D_CONV + Q_DIM + 2 * KV_DIM + D_MODEL]

kernel_name = "hybrid_conformer_swa_hmoe_step"

def rmsnorm(x, g):
    xf = x.astype(jnp.float32)
    y = xf * lax.rsqrt(jnp.mean(xf * xf, axis=-1, keepdims=True) + EPS)
    return (y * g.astype(jnp.float32)).astype(x.dtype)

def layernorm(x, g, b):
    xf = x.astype(jnp.float32)
    xc = xf - jnp.mean(xf, axis=-1, keepdims=True)
    var = jnp.mean(xc * xc, axis=-1, keepdims=True)
    y = xc * lax.rsqrt(var + EPS) * g.astype(jnp.float32) + b.astype(jnp.float32)
    return y.astype(x.dtype)

def t5_bucket(dist):
    n = jnp.maximum(dist, 0)
    nf = jnp.maximum(n, 1).astype(jnp.float32)
    large = MAX_EXACT + (jnp.log(nf / MAX_EXACT) / math.log(MAX_DISTANCE / MAX_EXACT)
                         * (N_BUCKETS - MAX_EXACT)).astype(jnp.int32)
    return jnp.where(n < MAX_EXACT, n, jnp.minimum(large, N_BUCKETS - 1))

def project(xn, w_in, q_norm_g, k_norm_g):
    lead = xn.shape[:-1]
    h = xn @ w_in
    a, b, q, k, v, ga, gb = jnp.split(h, SPLITS, axis=-1)
    glu = a * jax.nn.sigmoid(b)
    q = rmsnorm(q.reshape(lead + (N_KV_HEADS, GQA_GROUP, HEAD_DIM)), q_norm_g)
    k = rmsnorm(k.reshape(lead + (N_KV_HEADS, HEAD_DIM)), k_norm_g)
    v = v.reshape(lead + (N_KV_HEADS, HEAD_DIM))
    return glu, q, k, v, ga, gb

def conv_branch(glu_hist, w_dw, b_dw, conv_ln_g, conv_ln_b, w_conv_out, b_conv_out):
    y = lax.conv_general_dilated(glu_hist, w_dw[:, None, :], window_strides=(1,), padding='VALID',
                                 dimension_numbers=('NWC', 'WIO', 'NWC'),
                                 feature_group_count=D_CONV) + b_dw
    y = jax.nn.silu(layernorm(y, conv_ln_g, conv_ln_b))
    return y @ w_conv_out + b_conv_out

def window_attention(q, k, v, q_pos, k_pos, rel_bias, attn_sinks):
    s = jnp.einsum('...qkgd,...skd->...qskg', q, k).astype(jnp.float32) * (HEAD_DIM ** -0.5)
    dist = q_pos[..., :, None] - k_pos[..., None, :]
    valid = (dist >= 0) & (dist < WINDOW) & (k_pos[..., None, :] >= 0)
    bias = rel_bias.reshape(N_BUCKETS, N_KV_HEADS, GQA_GROUP)[t5_bucket(dist)].astype(jnp.float32)
    s = jnp.where(valid[..., None, None], s + bias, -jnp.inf)
    sink = jnp.broadcast_to(attn_sinks.reshape(N_KV_HEADS, GQA_GROUP).astype(jnp.float32),
                            s.shape[:-3] + (1,) + s.shape[-2:])
    p = jax.nn.softmax(jnp.concatenate([s, sink], axis=-3), axis=-3)[..., :-1, :, :]
    return jnp.einsum('...qskg,...skd->...qkgd', p.astype(v.dtype), v)

def hier_moe(xn, w_grp, b_grp, w_router, b_router, w_gate, w_up, w_down):
    t = xn.shape[0]
    g_logits = (xn @ w_grp).astype(jnp.float32) + b_grp.astype(jnp.float32)
    grp = jnp.argmax(g_logits, axis=-1)
    p_grp = jnp.take_along_axis(jax.nn.softmax(g_logits, axis=-1), grp[:, None], axis=-1)
    e_logits = ((xn @ w_router).astype(jnp.float32) + b_router.astype(jnp.float32)).reshape(
        t, N_GROUPS, EXPERTS_PER_GROUP)
    e_logits = jnp.take_along_axis(e_logits, grp[:, None, None], axis=1)[:, 0]
    top_p, top_i = lax.top_k(jax.nn.softmax(e_logits, axis=-1), TOP_K)
    weights = p_grp * top_p / jnp.sum(top_p, axis=-1, keepdims=True)
    eid = grp[:, None].astype(jnp.int32) * EXPERTS_PER_GROUP + top_i.astype(jnp.int32)
    n_pairs = t * TOP_K
    e_flat = eid.reshape(n_pairs)
    order = jnp.argsort(e_flat).astype(jnp.int32)
    e_sorted = e_flat[order]
    counts = jnp.bincount(e_flat, length=N_EXPERTS).astype(jnp.int32)
    starts = jnp.cumsum(counts) - counts
    pcounts = (counts + MOE_BLOCK - 1) // MOE_BLOCK * MOE_BLOCK
    pends = jnp.cumsum(pcounts)
    pstarts = pends - pcounts
    dest = pstarts[e_sorted] + jnp.arange(n_pairs, dtype=jnp.int32) - starts[e_sorted]
    n_blocks = -(-(n_pairs + N_EXPERTS * (MOE_BLOCK - 1)) // MOE_BLOCK)
    rows = n_blocks * MOE_BLOCK
    tok_buf = jnp.zeros((rows,), jnp.int32).at[dest].set(order // TOP_K)
    w_buf = jnp.zeros((rows,), jnp.float32).at[dest].set(weights.reshape(n_pairs)[order])
    blk_start = jnp.arange(n_blocks, dtype=jnp.int32) * MOE_BLOCK
    blk_expert = jnp.minimum(jnp.sum(blk_start[:, None] >= pends[None, :], axis=1), N_EXPERTS - 1)
    xb = xn[tok_buf].reshape(n_blocks, MOE_BLOCK, D_MODEL)

    def expert_block(args):
        xblk, e = args
        hid = jax.nn.silu(xblk @ w_gate[e]) * (xblk @ w_up[e])
        return hid @ w_down[e]

    yb = lax.map(expert_block, (xb, blk_expert)).reshape(rows, D_MODEL)
    return jnp.zeros_like(xn).at[tok_buf].add(yb * w_buf[:, None].astype(yb.dtype))

def finish_layer(x, conv_out, attn_o, ga, gb, w_attn_out, w_out, norm_ffn_g,
                 w_grp, b_grp, w_router, b_router, w_gate, w_up, w_down):
    bsz, t = x.shape[0], x.shape[1]
    attn_out = attn_o.reshape(bsz, t, Q_DIM) @ w_attn_out
    merged = jax.nn.sigmoid(ga) * conv_out + jax.nn.sigmoid(gb) * attn_out
    h = x + merged @ w_out
    hn = rmsnorm(h, norm_ffn_g).reshape(bsz * t, D_MODEL)
    return h + hier_moe(hn, w_grp, b_grp, w_router, b_router, w_gate, w_up, w_down).reshape(bsz, t, D_MODEL)

def setup_inputs(seed: int = 0) -> dict:
    key = jax.random.key(seed)
    ks = jax.random.split(key, 28)

    def nrm(k, shape, scale):
        return jax.random.normal(k, shape, jnp.float32) * scale

    return {
        "x_prompt": nrm(ks[0], (BATCH, SEQ, D_MODEL), 1.0),
        "x_sample": nrm(ks[1], (DEC_BATCH, DEC_SEQ, D_MODEL), 1.0),
        "state_conv": nrm(ks[2], (DEC_BATCH, CONV_WIDTH - 1, D_CONV), 0.5),
        "cache_k": nrm(ks[3], (DEC_BATCH, WINDOW, N_KV_HEADS, HEAD_DIM), 1.0),
        "cache_v": nrm(ks[4], (DEC_BATCH, WINDOW, N_KV_HEADS, HEAD_DIM), 1.0),
        "norm_attn_g": 1.0 + nrm(ks[5], (D_MODEL,), 0.05),
        "w_in": nrm(ks[6], (D_MODEL, IN_DIM), D_MODEL ** -0.5),
        "q_norm_g": 1.0 + nrm(ks[7], (HEAD_DIM,), 0.05),
        "k_norm_g": 1.0 + nrm(ks[8], (HEAD_DIM,), 0.05),
        "rel_bias": nrm(ks[9], (N_BUCKETS, N_HEADS), 0.5),
        "attn_sinks": nrm(ks[10], (N_HEADS,), 0.5),
        "w_dw": nrm(ks[11], (CONV_WIDTH, D_CONV), CONV_WIDTH ** -0.5),
        "b_dw": nrm(ks[12], (D_CONV,), 0.02),
        "conv_ln_g": 1.0 + nrm(ks[13], (D_CONV,), 0.05),
        "conv_ln_b": nrm(ks[14], (D_CONV,), 0.02),
        "w_conv_out": nrm(ks[15], (D_CONV, D_MODEL), D_CONV ** -0.5),
        "b_conv_out": nrm(ks[16], (D_MODEL,), 0.02),
        "w_attn_out": nrm(ks[17], (Q_DIM, D_MODEL), Q_DIM ** -0.5),
        "w_out": nrm(ks[18], (D_MODEL, D_MODEL), D_MODEL ** -0.5),
        "norm_ffn_g": 1.0 + nrm(ks[19], (D_MODEL,), 0.05),
        "w_grp": nrm(ks[20], (D_MODEL, N_GROUPS), D_MODEL ** -0.5),
        "b_grp": nrm(ks[21], (N_GROUPS,), 0.01),
        "w_router": nrm(ks[22], (D_MODEL, N_EXPERTS), D_MODEL ** -0.5),
        "b_router": nrm(ks[23], (N_EXPERTS,), 0.01),
        "w_gate": nrm(ks[24], (N_EXPERTS, D_MODEL, D_EXPERT), D_MODEL ** -0.5),
        "w_up": nrm(ks[25], (N_EXPERTS, D_MODEL, D_EXPERT), D_MODEL ** -0.5),
        "w_down": nrm(ks[26], (N_EXPERTS, D_EXPERT, D_MODEL), D_EXPERT ** -0.5),
    }

def reference(x_prompt, x_sample, state_conv, cache_k, cache_v, norm_attn_g, w_in, q_norm_g, k_norm_g,
              rel_bias, attn_sinks, w_dw, b_dw, conv_ln_g, conv_ln_b, w_conv_out, b_conv_out,
              w_attn_out, w_out, norm_ffn_g, w_grp, b_grp, w_router, b_router, w_gate, w_up, w_down):
    y_prompt = x_prompt
    y_sample = x_sample
    for _layer in range(DEPTH):
        bsz, t = y_prompt.shape[0], y_prompt.shape[1]
        xn = rmsnorm(y_prompt, norm_attn_g)
        glu, q, k, v, ga, gb = project(xn, w_in, q_norm_g, k_norm_g)
        glu_hist = jnp.concatenate([jnp.zeros((bsz, CONV_WIDTH - 1, D_CONV), glu.dtype), glu], axis=1)
        conv_out = conv_branch(glu_hist, w_dw, b_dw, conv_ln_g, conv_ln_b, w_conv_out, b_conv_out)
        nblk = t // ATTN_BLOCK
        qb = q.reshape(bsz, nblk, ATTN_BLOCK, N_KV_HEADS, GQA_GROUP, HEAD_DIM)
        kb = k.reshape(bsz, nblk, ATTN_BLOCK, N_KV_HEADS, HEAD_DIM)
        vb = v.reshape(bsz, nblk, ATTN_BLOCK, N_KV_HEADS, HEAD_DIM)
        k_band = jnp.concatenate([jnp.concatenate([jnp.zeros_like(kb[:, :1]), kb[:, :-1]], axis=1), kb], axis=2)
        v_band = jnp.concatenate([jnp.concatenate([jnp.zeros_like(vb[:, :1]), vb[:, :-1]], axis=1), vb], axis=2)
        q_pos = jnp.arange(t, dtype=jnp.int32).reshape(nblk, ATTN_BLOCK)
        k_pos = jnp.concatenate([q_pos - ATTN_BLOCK, q_pos], axis=-1)
        o = window_attention(qb, k_band, v_band, q_pos, k_pos, rel_bias, attn_sinks)
        o = o.reshape(bsz, t, N_KV_HEADS, GQA_GROUP, HEAD_DIM)
        y_prompt = finish_layer(y_prompt, conv_out, o, ga, gb, w_attn_out, w_out, norm_ffn_g,
                                w_grp, b_grp, w_router, b_router, w_gate, w_up, w_down)
        state_conv_prompt = glu_hist[:, -(CONV_WIDTH - 1):]
        cache_k_prompt = k[:, -WINDOW:]
        cache_v_prompt = v[:, -WINDOW:]

        xn = rmsnorm(y_sample, norm_attn_g)
        glu, q, k, v, ga, gb = project(xn, w_in, q_norm_g, k_norm_g)
        glu_hist = jnp.concatenate([state_conv.astype(glu.dtype), glu], axis=1)
        conv_out = conv_branch(glu_hist, w_dw, b_dw, conv_ln_g, conv_ln_b, w_conv_out, b_conv_out)
        k_all = jnp.concatenate([cache_k.astype(k.dtype), k], axis=1)
        v_all = jnp.concatenate([cache_v.astype(v.dtype), v], axis=1)
        q_pos = PAST_LEN + jnp.arange(y_sample.shape[1], dtype=jnp.int32)
        k_pos = jnp.concatenate([PAST_LEN - WINDOW + jnp.arange(WINDOW, dtype=jnp.int32), q_pos])
        o = window_attention(q, k_all, v_all, q_pos, k_pos, rel_bias, attn_sinks)
        y_sample = finish_layer(y_sample, conv_out, o, ga, gb, w_attn_out, w_out, norm_ffn_g,
                                w_grp, b_grp, w_router, b_router, w_gate, w_up, w_down)
        state_conv_sample = glu_hist[:, -(CONV_WIDTH - 1):]
        cache_k_sample = k_all[:, -WINDOW:]
        cache_v_sample = v_all[:, -WINDOW:]
    return (y_prompt, y_sample, state_conv_prompt, cache_k_prompt, cache_v_prompt,
            state_conv_sample, cache_k_sample, cache_v_sample)


_drawn_inputs = setup_inputs


def setup_inputs(seed=0):
    import zlib

    import numpy as np

    out = dict(_drawn_inputs(seed))
    spreads = {}
    factors = {'q_norm_g': 2.931,
     'attn_sinks': 7.774,
     'conv_ln_b': 3.376,
     'b_grp': 23.667,
     'b_router': 2.704}
    for name, (base, spread) in spreads.items():
        noise = np.random.default_rng([zlib.crc32(name.encode()), seed]).standard_normal(out[name].shape)
        drawn = base * np.exp(spread * noise) if base else spread * noise
        out[name] = jnp.asarray(drawn.astype(out[name].dtype))
    for name, factor in factors.items():
        out[name] = (out[name] * factor).astype(out[name].dtype)
    return out
```

```python
from contextlib import ExitStack

import numpy as np
import concourse.bass as bass
from concourse import mybir

F32 = mybir.dt.float32
F16 = mybir.dt.float16
I32 = mybir.dt.int32
U32 = mybir.dt.uint32
ALU = mybir.AluOpType
ACT = mybir.ActivationFunctionType
AX = mybir.AxisListType
ds = bass.ds

P = 128
D = 1024
KC = D // P
SEQ = 1024
NSEQ, DSEQ = 8, 8
T = SEQ + NSEQ * DSEQ
NT = SEQ // P
TT = NT + 1
TP = TT * P
THIRD = 364
TM = 3 * THIRD
TS = NSEQ * DSEQ
HD, NH, NKV = 64, 16, 4
GQ = NH // NKV
KVW = NKV * HD
QKVW = D + 2 * KVW
WIN = 128
NB = 32
RW = 383
COPIES = 32
TAPS = 31
HIST = TAPS - 1
SLEN = HIST + DSEQ
GLU_W = HIST + SEQ + NSEQ * SLEN
COL_A, COL_B, COL_Q, COL_GA, COL_GB = 0, D, 2 * D, 2 * D + QKVW, 3 * D + QKVW
IN_DIM = 4 * D + QKVW
NG, EPG = 4, 8
NE = NG * EPG
RT = NG + NE
DE = 256
BLK = 128
NBLK = (2 * T + NE * (BLK - 1)) // BLK
EPS = 1e-6
NEG = -1.0e30
S_X, S_W, S_H = 64.0, 128.0, 32.0
UNSCALE = 1.0 / (S_X * S_W)


class OnChip:
    pass


def mm3(pe, out, stat, mov, start, stop):
    pe.matmul(out, stat[0], mov[0], start=start, stop=False)
    pe.matmul(out, stat[0], mov[1], start=False, stop=False)
    return pe.matmul(out, stat[1], mov[0], start=False, stop=stop)


def rows_on_partitions(ap, count, width):
    return bass.AP(tensor=ap.tensor, offset=ap.offset, ap=[[0, count], [1, width]])


def high_weights(g):
    return g.big[:, 0:KC * QKVW // 2].bitcast(F16).rearrange("p (k n) -> p k n", k=KC)


def norm_phase(nc, sem, g, A):
    with ExitStack() as c:
        def sb(name, shape, dt):
            return c.enter_context(nc.sbuf_tensor(name, shape, dt))

        x_in = sb("n_x", [P, 2, D], F32)
        xg = sb("n_xg", [P, 2, D], F32)
        junk = sb("n_junk", [P, D], F32)
        gain = sb("n_gain", [P, D], F32)
        ss = sb("n_ss", [P, 1], F32)
        ms = sb("n_ms", [P, 1], F32)
        rstd = sb("n_rstd", [P, 1], F32)
        xT = c.enter_context(nc.psum_tensor("n_xT", [P, 2, KC, P], F32))
        const_ld, gain_ld, x_ld0, x_ld = sem("n_const_ld"), sem("n_gain_ld"), sem("n_x_ld0"), sem("n_x_ld")
        w_ld0, w_ld, w_high, w_low = sem("n_w_ld0"), sem("n_w_ld"), sem("n_w_high"), sem("n_w_low")
        half_done, sum_done, mean_done, rstd_done = sem("n_half"), sem("n_sum"), sem("n_mean"), sem("n_rstd")
        xg_done, xT_done, high_done, xT_free = sem("n_xg"), sem("n_xT"), sem("n_high"), sem("n_xT_free")
        block = c.enter_context(nc.Block())

        def slot(buf, t):
            return buf[:, ds(t % 2, 1), :].rearrange("p a n -> p (a n)")

        w_h = high_weights(g)

        def row(buf, k):
            return buf[:, ds(k, 1), :].rearrange("p a n -> p (a n)")

        def slot_T(t):
            return xT[:, ds(t % 2, 1)].rearrange("p a k n -> p (a k) n")

        @block.sync
        def _(sp):
            sp.dma_start(x_in[:, 0, :], A["x_all"][0:P, :]).then_inc(x_ld0, 16)
            sp.dma_start(gain[:], rows_on_partitions(A["norm_attn_g"], P, D)).then_inc(gain_ld, 16)
            sp.dma_start(g.ident[:], A["c_ident"]).then_inc(const_ld, 16)
            sp.dma_start(g.qkv[:, 0], A["w_in"][0:P, COL_Q:COL_Q + QKVW]).then_inc(w_ld0, 16)

            def load_x(t):
                sp.wait_ge(x_ld, 16 * t)
                sp.wait_ge(xg_done, t)
                sp.dma_start(slot(x_in, t + 1), A["x_all"][ds((t + 1) * P, P), :]).then_inc(x_ld, 16)

            with sp.Fori(0, KC - 1) as t:
                load_x(t)
                sp.wait_ge(w_ld, 16 * t)
                sp.wait_ge(w_low, t)
                sp.dma_start(slot(g.qkv, t + 1), A["w_in"][ds((t + 1) * P, P), COL_Q:COL_Q + QKVW]).then_inc(w_ld, 16)
            with sp.Fori(KC - 1, TT - 1) as t:
                load_x(t)

        @block.scalar
        def _(act):
            def squares(t):
                act.wait_ge(x_ld, 16 * t)
                act.wait_ge(mean_done, t)
                act.activation(junk[:], slot(x_in, t), ACT.Square, accum_out=ss[:]).then_inc(sum_done, 1)

            def turned(t):
                act.wait_ge(xT_done, t + 1)
                act.activation(g.xnT_h[:, :, ds(t * P, P)], slot_T(t), ACT.Copy, scale=S_X).then_inc(high_done, 1)

            act.wait_ge(x_ld0, 16)
            act.activation(junk[:], x_in[:, 0, :], ACT.Square, accum_out=ss[:]).then_inc(sum_done, 1)
            act.wait_ge(w_ld0, 16)
            with act.Fori(0, KC) as t:
                squares(t + 1)
                act.wait_ge(w_ld, 16 * t)
                act.activation(row(w_h, t), slot(g.qkv, t), ACT.Copy, scale=S_W).then_inc(w_high, 1)
                turned(t)
            turned(TT - 1)

        @block.gpsimd
        def _(pool):
            pool.memset(g.neg_half[:], -0.5).then_inc(half_done, 1)
            pool.wait_ge(half_done, 1)
            with pool.Fori(0, TT) as t:
                pool.wait_ge(mean_done, t + 1)
                pool.wait_ge(xg_done, t)
                pool.tensor_tensor(rstd[:], ms[:], g.neg_half[:, 0:1], ALU.pow).then_inc(rstd_done, 1)

        @block.vector
        def _(dve):
            dve.sem_inc(xT_free, 2)
            dve.wait_ge(gain_ld, 16)

            def scale_tile(t):
                dve.wait_ge(sum_done, t + 1)
                dve.tensor_scalar(ms[:], ss[:], 1.0 / D, EPS, ALU.mult, ALU.add).then_inc(mean_done, 1)
                dve.wait_ge(rstd_done, t + 1)
                dve.scalar_tensor_tensor(slot(xg, t), slot(x_in, t), rstd[:, 0:1], gain[:],
                                         op0=ALU.mult, op1=ALU.mult).then_inc(xg_done, 1)

            def low_part(t):
                dve.wait_ge(high_done, t + 1)
                dve.scalar_tensor_tensor(g.xnT_l[:, :, ds(t * P, P)], slot_T(t), S_X, g.xnT_h[:, :, ds(t * P, P)],
                                         op0=ALU.mult, op1=ALU.subtract).then_inc(xT_free, 1)

            scale_tile(0)
            with dve.Fori(0, KC) as t:
                scale_tile(t + 1)
                dve.wait_ge(w_high, t + 1)
                dve.scalar_tensor_tensor(row(g.w_qkv_l, t), slot(g.qkv, t), S_W, row(w_h, t), op0=ALU.mult,
                                         op1=ALU.subtract).then_inc(w_low, 1)
                low_part(t)
            low_part(TT - 1)

        @block.tensor
        def _(pe):
            def transpose_tile(t, par):
                pe.wait_ge(xg_done, t + 1)
                pe.wait_ge(xT_free, t + 1)
                for k in range(KC):
                    last = pe.transpose(xT[:, par, k, :], xg[:, par, k * P:(k + 1) * P], g.ident[:])
                last.then_inc(xT_done, 1)

            pe.wait_ge(const_ld, 16)
            with pe.Fori(0, TT // 2) as u:
                transpose_tile(2 * u, 0)
                transpose_tile(2 * u + 1, 1)
            transpose_tile(TT - 1, (TT - 1) % 2)


def attention_phase(nc, sem, g, A):
    with ExitStack() as c:
        def sb(name, shape, dt):
            return c.enter_context(nc.sbuf_tensor(name, shape, dt))

        def ps(name, shape, dt):
            return c.enter_context(nc.psum_tensor(name, shape, dt))

        w_h, w_l = high_weights(g), g.w_qkv_l
        rel = sb("a_rel", [NB, NH], F32)
        bucket = sb("a_bucket", [NB, RW], F32)
        mask = sb("a_mask", [NH, RW], F32)
        by_dist = sb("a_by_dist", [NH, RW], F32)
        bias = sb("a_bias", [P, NH, 2 * P], F32)
        nsink = sb("a_nsink", [P, NH], F32)
        gq = sb("a_gq", [P, 1], F32)
        gq64 = sb("a_gq64", [P, 1], F32)
        gk = sb("a_gk", [P, HD], F32)
        qkv = g.qkv
        sq = sb("a_sq", [P, D + KVW], F32)
        ss = sb("a_ss", [P, NH + NKV], F32)
        ms = sb("a_ms", [P, NH + NKV], F32)
        rs = sb("a_rs", [P, NH + NKV], F32)
        qn = g.q_s
        kn = sb("a_kn", [P, 2, KVW], F32)
        k2 = sb("a_k2", [P, NKV, 2, HD], F32)
        qT_h = sb("a_qT_h", [P, KC, P], F16)
        qT_l = sb("a_qT_l", [P, KC, P], F16)
        kz_h = sb("a_kz_h", [P, 2, 2, NKV, P], F16)
        kz_l = sb("a_kz_l", [P, 2, 2, NKV, P], F16)
        v_h = sb("a_v_h", [P, 2, KVW], F16)
        v_l = sb("a_v_l", [P, 2, KVW], F16)
        prob = g.big[:, KC * QKVW // 2:KC * QKVW // 2 + 4 * GQ * P].rearrange("p (a r n) -> p a r n", a=2, r=GQ)
        top = sb("a_top", [P, 2, GQ], F32)
        ntop = sb("a_ntop", [P, 2, GQ], F32)
        sk = sb("a_sk", [P, 2, GQ], F32)
        esk = sb("a_esk", [P, 2, GQ], F32)
        den = sb("a_den", [P, 2, GQ], F32)
        dent = sb("a_dent", [P, 2, GQ], F32)
        rden = sb("a_rden", [P, 2, GQ], F32)
        pT_h = sb("a_pT_h", [P, 2, KC, P], F16)
        pT_l = sb("a_pT_l", [P, 2, KC, P], F16)
        o_n = sb("a_o", [P, D], F32)
        psS = ps("a_psS", [P, 2, GQ, 2 * P], F32)
        psT = ps("a_psT", [P, KC, P], F32)
        psP = ps("a_psP", [P, 512], F32)
        psO = ps("a_psO", [P, NKV, P], F32)

        cst_ld, msk_ld, gq_ld, gk_ld, snk_ld = sem("a_cst"), sem("a_msk"), sem("a_gq"), sem("a_gk"), sem("a_snk")
        dist_mm, dist_done, dist_st, bias_ld, sbias_ld, ssnk_ld = (
            sem("a_dist_mm"), sem("a_dist"), sem("a_dist_st"), sem("a_bias_ld"), sem("a_sbias"), sem("a_ssnk"))
        ck_ld, cv_ld, ck_st, cv_st, out_st, vn_ld = (
            sem("a_ck_ld"), sem("a_cv_ld"), sem("a_ck_st"), sem("a_cv_st"), sem("a_out_st"), sem("a_vn_ld"))
        setup_done = sem("a_setup")
        proj_done, proj_free = sem("a_proj"), sem("a_proj_free")
        sq_done, ss_done, ms_done, rs_done = sem("a_sq"), sem("a_ss"), sem("a_ms"), sem("a_rs")
        qn_done, kn_done, k2_done = sem("a_qn"), sem("a_kn"), sem("a_k2")
        T_done, T_high, T_free = sem("a_T"), sem("a_T_high"), sem("a_T_free")
        kT_done, kv_high, kv_low = sem("a_kT"), sem("a_kv_high"), sem("a_kv_low")
        s_done, s_free = sem("a_s"), sem("a_s_free")
        top_done, ntop_done, sk_done, exp_done, esk_done = (
            sem("a_top"), sem("a_ntop"), sem("a_sk"), sem("a_exp"), sem("a_esk"))
        dent_done, rden_done = sem("a_dent"), sem("a_rden")
        o_done, o_norm = sem("a_o"), sem("a_o_norm")
        block = c.enter_context(nc.Block())

        def slot(buf, t):
            if isinstance(t, int):
                return buf[:, t % 2]
            return buf[:, ds(t % 2, 1)].rearrange("p a n -> p (a n)")

        def kz_slot(buf, t, half, grp):
            if isinstance(t, int):
                return buf[:, t % 2, half, grp]
            return buf[:, ds(t % 2, 1), half, grp].rearrange("p a n -> p (a n)")

        def use_q(t):
            return 0 if isinstance(t, int) and t == 0 else 6 * t - 1

        def use_o(t):
            return 6 * t

        def use_p(t, grp):
            return 6 * t + 1 + grp

        @block.sync
        def _(sp):
            sp.dma_start(rel[:], A["rel_bias"]).then_inc(cst_ld, 16)
            sp.dma_start(bucket[:], A["c_bucket"]).then_inc(msk_ld, 16)
            sp.dma_start(mask[:], A["c_mask"]).then_inc(gq_ld, 16)
            sp.dma_start(gq[:], A["gq2"]).then_inc(gk_ld, 16)
            sp.dma_start(A["ck_sample"][:, 0:WIN - DSEQ, :], A["cache_k"][:, DSEQ:WIN, :]).then_inc(ck_st, 16)
            sp.dma_start(A["cv_sample"][:, 0:WIN - DSEQ, :], A["cache_v"][:, DSEQ:WIN, :]).then_inc(cv_st, 16)
            sp.wait_ge(kn_done, NT)
            sp.dma_start(A["ck_prompt"], kn[:, (NT - 1) % 2, :]).then_inc(out_st, 16)
            sp.dma_start(A["cv_prompt"], qkv[:, (NT - 1) % 2, D + KVW:QKVW]).then_inc(cv_st, 16)
            sp.wait_ge(ck_st, 16)
            sp.wait_ge(cv_st, 32)
            sp.wait_ge(out_st, 16)

        @block.gpsimd
        def _(pool):
            pool.dma_start(gk[:], rows_on_partitions(A["k_norm_g"], P, HD)).then_inc(snk_ld, 16)
            pool.dma_start(nsink[:], rows_on_partitions(A["attn_sinks"], P, NH)).then_inc(snk_ld, 16)
            pool.wait_ge(dist_done, 1)
            pool.dma_start(A["dist_dram"].rearrange("(c h) r -> h c r", h=NH),
                           by_dist[:].unsqueeze(1).to_broadcast([NH, COPIES, RW])).then_inc(dist_st, 16)
            pool.wait_ge(dist_st, 16)
            for i0 in range(0, P, COPIES):
                pool.dma_start(bias[i0:i0 + COPIES],
                               bass.AP(tensor=A["dist_dram"].tensor, offset=P - 1 - i0,
                                       ap=[[NH * RW - 1, COPIES], [RW, NH], [1, 2 * P]])).then_inc(bias_ld, 16)
            def root(t):
                pool.wait_ge(ms_done, t + 1)
                pool.wait_ge(k2_done, t)
                pool.tensor_tensor(rs[:], ms[:], g.neg_half[:, 0:NH + NKV], ALU.pow).then_inc(rs_done, 1)

            with pool.Fori(0, TT) as t:
                root(t)

        @block.scalar
        def _(act):
            def piece(t, nb):
                act.wait_ge(proj_done, 3 * t + nb + 1)
                act.activation(slot(qkv, t)[:, nb * 512:(nb + 1) * 512], psP[:], ACT.Copy,
                               scale=UNSCALE).then_inc(proj_free, 1)

            def squares(t):
                act.wait_ge(ss_done, t)
                act.wait_ge(proj_free, 3 * t + 3)
                act.activation(sq[:, KVW:], slot(qkv, t)[:, KVW:D + KVW], ACT.Square)
                act.activation(sq[:, 0:KVW], slot(qkv, t)[:, 0:KVW], ACT.Square).then_inc(sq_done, 1)

            def turned(dst, use):
                act.wait_ge(T_done, use + 1)
                act.activation(dst, psT[:], ACT.Copy, scale=S_X).then_inc(T_high, 1)

            def split_qkv(t):
                act.wait_ge(T_done, use_q(t) + 1)
                act.activation(qT_h[:], psT[:], ACT.Copy, scale=gq64[:, 0:1]).then_inc(T_high, 1)
                act.wait_ge(kT_done, t + 1)
                act.wait_ge(o_done, 4 * t)
                for half in range(2):
                    r = slice(half * HD, (half + 1) * HD)
                    dst = kz_h[r, ds(t % 2, 1), half].rearrange("p a k n -> p (a k) n")
                    act.activation(dst, psO[r], ACT.Copy, scale=S_X).then_inc(kv_high, 1)
                act.activation(slot(v_h, t), slot(qkv, t)[:, D + KVW:QKVW], ACT.Copy, scale=S_X).then_inc(kv_high, 1)

            def exps(t, grp, lo):
                n, s = 4 * t + grp, grp % 2
                act.wait_ge(ntop_done, n + 1)
                for r in range(GQ):
                    act.activation(prob[:, s, r, lo:], prob[:, s, r, lo:], ACT.Exp, bias=ntop[:, s, r:r + 1],
                                   accum_out=den[:, s, r:r + 1]).then_inc(exp_done, 1)
                act.wait_ge(sk_done, n + 1)
                act.activation(esk[:, s], sk[:, s], ACT.Exp).then_inc(esk_done, 1)

            act.wait_ge(setup_done, 2)
            for nb in range(3):
                piece(0, nb)
            squares(0)

            def turned_p(t, grp, first):
                if not first or grp > 1:
                    act.wait_ge(o_done, 4 * t + grp - 1)
                n = GQ if first else KC
                act.wait_ge(T_done, use_p(t, grp) + 1)
                act.activation(pT_h[:, grp % 2, 0:n], psT[:, 0:n], ACT.Copy, scale=S_X).then_inc(T_high, 1)

            def tile(t, first):
                lo = P if first else 0
                split_qkv(t)
                piece(t + 1, 0)
                if not first:
                    turned(g.oT_h[:, :, ds((t - 1) * P, P)], use_o(t))
                exps(t, 0, lo)
                piece(t + 1, 1)
                turned_p(t, 0, first)
                exps(t, 1, lo)
                piece(t + 1, 2)
                squares(t + 1)
                turned_p(t, 1, first)
                exps(t, 2, lo)
                turned_p(t, 2, first)
                exps(t, 3, lo)
                turned_p(t, 3, first)

            tile(0, True)
            with act.Fori(1, NT) as t:
                tile(t, False)
            turned(g.oT_h[:, :, (NT - 1) * P:NT * P], use_q(NT))

        @block.vector
        def _(dve):
            dve.memset(kz_h[:], 0.0).then_inc(setup_done, 1)
            dve.memset(kz_l[:], 0.0).then_inc(setup_done, 1)
            dve.memset(g.oT_h[:, :, T:TP], 0.0).then_inc(setup_done, 1)
            dve.memset(g.oT_l[:, :, T:TP], 0.0).then_inc(setup_done, 1)
            dve.wait_ge(gk_ld, 16)
            dve.tensor_scalar(gq64[:], gq[:], S_X, None, ALU.mult).then_inc(setup_done, 1)
            dve.wait_ge(dist_mm, 1)
            dve.tensor_tensor(by_dist[:], psP[0:NH, 0:RW], mask[:], ALU.add).then_inc(dist_done, 1)
            dve.wait_ge(snk_ld, 32)
            dve.tensor_scalar(nsink[:], nsink[:], -1.0, None, ALU.mult).then_inc(setup_done, 1)

            def mean_squares(t):
                dve.wait_ge(sq_done, t + 1)
                dve.tensor_reduce(ss[:], sq[:].rearrange("p (h d) -> p h d", d=HD), AX.X, ALU.add).then_inc(ss_done, 1)
                dve.wait_ge(ss_done, t + 1)
                dve.tensor_scalar(ms[:], ss[:], 1.0 / HD, EPS, ALU.mult, ALU.add).then_inc(ms_done, 1)

            def norms(t):
                dve.wait_ge(rs_done, t + 1)
                dve.tensor_tensor(qn[:].rearrange("p (h d) -> p h d", d=HD),
                                  slot(qkv, t)[:, 0:D].rearrange("p (h d) -> p h d", d=HD),
                                  rs[:, 0:NH].unsqueeze(2).to_broadcast([P, NH, HD]), ALU.mult).then_inc(qn_done, 1)
                dve.tensor_tensor(slot(kn, t).rearrange("p (h d) -> p h d", d=HD),
                                  slot(qkv, t)[:, D:D + KVW].rearrange("p (h d) -> p h d", d=HD),
                                  rs[:, NH:].unsqueeze(2).to_broadcast([P, NKV, HD]), ALU.mult).then_inc(qn_done, 1)
                dve.wait_ge(qn_done, 2 * t + 2)
                dve.tensor_tensor(slot(kn, t).rearrange("p (h d) -> p h d", d=HD), slot(kn, t).rearrange("p (h d) -> p h d", d=HD),
                                  gk[:].unsqueeze(1).to_broadcast([P, NKV, HD]), ALU.mult).then_inc(kn_done, 1)
                dve.wait_ge(kn_done, t + 1)
                dve.tensor_scalar(k2[:], slot(kn, t).rearrange("p (h d) -> p h d", d=HD).unsqueeze(2)
                                  .to_broadcast([P, NKV, 2, HD]), 1.0, None, ALU.mult).then_inc(k2_done, 1)

            def low_turned(dst, high, use):
                dve.wait_ge(T_high, use + 1)
                dve.scalar_tensor_tensor(dst, psT[:, 0:dst.shape[1]], S_X, high, op0=ALU.mult,
                                         op1=ALU.subtract).then_inc(T_free, 1)

            def split_qkv(t):
                dve.wait_ge(T_high, use_q(t) + 1)
                dve.scalar_tensor_tensor(qT_l[:], psT[:], gq64[:, 0:1], qT_h[:], op0=ALU.mult,
                                         op1=ALU.subtract).then_inc(T_free, 1)
                dve.wait_ge(kv_high, 3 * t + 3)
                for half in range(2):
                    r = slice(half * HD, (half + 1) * HD)
                    dve.scalar_tensor_tensor(kz_l[r, ds(t % 2, 1), half].rearrange("p a k n -> p (a k) n"), psO[r], S_X,
                                             kz_h[r, ds(t % 2, 1), half].rearrange("p a k n -> p (a k) n"),
                                             op0=ALU.mult, op1=ALU.subtract).then_inc(kv_low, 1)
                dve.scalar_tensor_tensor(slot(v_l, t), slot(qkv, t)[:, D + KVW:QKVW], S_X, slot(v_h, t),
                                         op0=ALU.mult, op1=ALU.subtract).then_inc(kv_low, 1)

            def logits(t, grp, lo):
                n, s = 4 * t + grp, grp % 2
                dve.wait_ge(s_done, n + 1)
                dve.scalar_tensor_tensor(prob[:, s, :, lo:], psS[:, s, :, lo:], 1.0 / (S_X * S_X * 8.0),
                                         bias[:, grp * GQ:(grp + 1) * GQ, lo:], op0=ALU.mult,
                                         op1=ALU.add).then_inc(s_free, 1)
                dve.wait_ge(s_free, n + 1)
                dve.tensor_reduce(top[:, s], prob[:, s, :, lo:], AX.X, ALU.max).then_inc(top_done, 1)
                dve.wait_ge(top_done, n + 1)
                dve.scalar_tensor_tensor(ntop[:, s], top[:, s], -1.0, nsink[:, grp * GQ:(grp + 1) * GQ],
                                         op0=ALU.mult, op1=ALU.min).then_inc(ntop_done, 1)
                dve.wait_ge(ntop_done, n + 1)
                dve.tensor_tensor(sk[:, s], ntop[:, s], nsink[:, grp * GQ:(grp + 1) * GQ],
                                  ALU.subtract).then_inc(sk_done, 1)

            def denominator(t, grp):
                n, s = 4 * t + grp, grp % 2
                dve.wait_ge(exp_done, 4 * n + 4)
                dve.wait_ge(esk_done, n + 1)
                dve.tensor_tensor(dent[:, s], den[:, s], esk[:, s], ALU.add).then_inc(dent_done, 1)
                dve.wait_ge(dent_done, n + 1)
                dve.reciprocal(rden[:, s], dent[:, s]).then_inc(rden_done, 1)

            def output(t, grp):
                n, s = 4 * t + grp, grp % 2
                dve.wait_ge(rden_done, n + 1)
                dve.wait_ge(o_done, n + 1)
                dve.scalar_tensor_tensor(o_n[:, grp * KVW:(grp + 1) * KVW].rearrange("p (r d) -> p r d", d=HD),
                                         psO[:, :, 0:HD], 1.0 / (S_X * S_X),
                                         rden[:, s].unsqueeze(2).to_broadcast([P, GQ, HD]), op0=ALU.mult,
                                         op1=ALU.mult).then_inc(o_norm, 1)

            mean_squares(0)
            norms(0)

            def tile(t, first):
                lo = P if first else 0
                n = GQ if first else KC

                def low_p(grp):
                    if not first or grp > 1:
                        dve.wait_ge(o_done, 4 * t + grp - 1)
                    low_turned(pT_l[:, grp % 2, 0:n], pT_h[:, grp % 2, 0:n], use_p(t, grp))

                split_qkv(t)
                if not first:
                    low_turned(g.oT_l[:, :, ds((t - 1) * P, P)], g.oT_h[:, :, ds((t - 1) * P, P)], use_o(t))
                logits(t, 0, lo)
                logits(t, 1, lo)
                denominator(t, 0)
                low_p(0)
                logits(t, 2, lo)
                denominator(t, 1)
                low_p(1)
                output(t, 0)
                logits(t, 3, lo)
                mean_squares(t + 1)
                denominator(t, 2)
                low_p(2)
                output(t, 1)
                denominator(t, 3)
                low_p(3)
                output(t, 2)
                norms(t + 1)
                output(t, 3)

            dve.wait_ge(bias_ld, 16 * (P // COPIES))
            dve.wait_ge(setup_done, 6)
            tile(0, True)
            with dve.Fori(1, NT) as t:
                tile(t, False)

            low_turned(g.oT_l[:, :, (NT - 1) * P:NT * P], g.oT_h[:, :, (NT - 1) * P:NT * P], use_q(NT))
            dve.wait_ge(kn_done, TT)
            dve.tensor_copy(g.v_s[:], qkv[:, NT % 2, D + KVW:QKVW]).then_inc(setup_done, 1)
            dve.tensor_copy(g.k_s[:], kn[:, NT % 2, :]).then_inc(setup_done, 1)

        @block.tensor
        def _(pe):
            pe.wait_ge(cst_ld, 16)
            pe.wait_ge(msk_ld, 16)
            pe.wait_ge(gq_ld, 16)
            pe.matmul(psP[0:NH, 0:RW], rel[:], bucket[:], start=True, stop=True).then_inc(dist_mm, 1)
            pe.wait_ge(dist_done, 1)

            def piece(t, nb):
                pe.wait_ge(proj_free, 3 * t + nb)
                cols = slice(nb * 512, (nb + 1) * 512)
                for k in range(KC):
                    last = mm3(pe, psP[:], (g.xnT_h[:, k, ds(t * P, P)], g.xnT_l[:, k, ds(t * P, P)]),
                               (w_h[:, k, cols], w_l[:, k, cols]), k == 0, k == KC - 1)
                last.then_inc(proj_done, 1)

            def turn_qk(t):
                pe.wait_ge(T_free, use_q(t))
                pe.wait_ge(qn_done, 2 * t + 2)
                for k in range(KC):
                    last = pe.transpose(psT[:, k, :], qn[:, k * P:(k + 1) * P], g.ident[:])
                last.then_inc(T_done, 1)
                pe.wait_ge(o_norm, 4 * t)
                pe.wait_ge(k2_done, t + 1)
                for grp in range(NKV):
                    last = pe.transpose(psO[:, grp, :], k2[:, grp].rearrange("p a d -> p (a d)"), g.ident[:])
                last.then_inc(kT_done, 1)

            def scores(t, grp, first):
                n, s = 4 * t + grp, grp % 2
                if grp == 0:
                    pe.wait_ge(T_free, use_q(t) + 1)
                    pe.wait_ge(kv_low, 3 * t + 3)
                if not (first and grp < 2):
                    pe.wait_ge(s_free, n - 1)
                for r in range(GQ):
                    h = grp * GQ + r
                    stat = (qT_h[:, h // 2, :], qT_l[:, h // 2, :])
                    for own in range(1 if first else 0, 2):
                        tk = t if own else t - 1
                        last = mm3(pe, psS[:, s, r, own * P:(own + 1) * P], stat,
                                   (kz_slot(kz_h, tk, h % 2, grp), kz_slot(kz_l, tk, h % 2, grp)), True, True)
                last.then_inc(s_done, 1)

            def turn_o(t):
                pe.wait_ge(T_free, use_o(t))
                pe.wait_ge(o_norm, 4 * t)
                for k in range(KC):
                    last = pe.transpose(psT[:, k, :], o_n[:, k * P:(k + 1) * P], g.ident[:])
                last.then_inc(T_done, 1)

            def turn_p(t, grp, first):
                n, s = 4 * t + grp, grp % 2
                pe.wait_ge(T_free, use_p(t, grp))
                pe.wait_ge(exp_done, 4 * n + 4)
                if first:
                    for r in range(GQ):
                        last = pe.transpose(psT[:, r, :], prob[:, s, r, P:], g.ident[:])
                else:
                    for r in range(GQ):
                        for own in range(2):
                            last = pe.transpose(psT[:, 2 * r + own, :], prob[:, s, r, own * P:(own + 1) * P],
                                                g.ident[:])
                last.then_inc(T_done, 1)

            def values(t, grp, first):
                n = 4 * t + grp
                pe.wait_ge(T_free, use_p(t, grp) + 1)
                if not first or grp > 0:
                    pe.wait_ge(o_norm, n)
                for r in range(GQ):
                    for own in range(1 if first else 0, 2):
                        tk = t if own else t - 1
                        j = r if first else 2 * r + own
                        last = mm3(pe, psO[:, r, 0:HD], (pT_h[:, grp % 2, j, :], pT_l[:, grp % 2, j, :]),
                                   (slot(v_h, tk)[:, grp * HD:(grp + 1) * HD],
                                    slot(v_l, tk)[:, grp * HD:(grp + 1) * HD]), own == 0 or first, own == 1)
                last.then_inc(o_done, 1)

            def tile(t, first):
                turn_qk(t)
                piece(t + 1, 0)
                scores(t, 0, first)
                if not first:
                    turn_o(t)
                scores(t, 1, first)
                piece(t + 1, 1)
                turn_p(t, 0, first)
                scores(t, 2, first)
                piece(t + 1, 2)
                turn_p(t, 1, first)
                values(t, 0, first)
                scores(t, 3, first)
                turn_p(t, 2, first)
                values(t, 1, first)
                turn_p(t, 3, first)
                values(t, 2, first)
                values(t, 3, first)

            for nb in range(3):
                piece(0, nb)
            tile(0, True)
            with pe.Fori(1, NT) as t:
                tile(t, False)

            pe.wait_ge(T_free, use_q(NT))
            pe.wait_ge(o_norm, 4 * NT)
            for k in range(KC):
                last = pe.transpose(psT[:, k, :], o_n[:, k * P:(k + 1) * P], g.ident[:])
            last.then_inc(T_done, 1)


def sample_phase(nc, sem, g, A):
    with ExitStack() as c:
        def sb(name, shape, dt):
            return c.enter_context(nc.sbuf_tensor(name, shape, dt))

        def ps(name, shape, dt):
            return c.enter_context(nc.psum_tensor(name, shape, dt))

        s_kT = sb("s_kT", [HD, NKV * NSEQ, WIN + DSEQ], F32)
        s_kT_h = sb("s_kT_h", [HD, NKV * NSEQ, WIN + DSEQ], F16)
        s_kT_l = sb("s_kT_l", [HD, NKV * NSEQ, WIN + DSEQ], F16)
        s_v = sb("s_v", [P, NSEQ, KVW], F32)
        s_v_h = sb("s_v_h", [P, NSEQ, KVW], F16)
        s_v_l = sb("s_v_l", [P, NSEQ, KVW], F16)
        s_vn = sb("s_vn", [DSEQ, NSEQ, KVW], F32)
        s_vn_h = sb("s_vn_h", [DSEQ, NSEQ, KVW], F16)
        s_vn_l = sb("s_vn_l", [DSEQ, NSEQ, KVW], F16)
        s_bias = sb("s_bias", [P, NKV, WIN + DSEQ], F32)
        s_nsink = sb("s_nsink", [P, NKV], F32)
        s_qT_h = sb("s_qT_h", [HD, NSEQ, NH, DSEQ], F16)
        s_qT_l = sb("s_qT_l", [HD, NSEQ, NH, DSEQ], F16)
        SU = 2 * NKV
        s_p = sb("s_p", [P, SU, WIN + DSEQ], F32)
        s_st = sb("s_st", [P, 8, SU], F32)
        s_pT_h = sb("s_pT_h", [P, SU, P], F16)
        s_pT_l = sb("s_pT_l", [P, SU, P], F16)
        s_pnT_h = sb("s_pnT_h", [DSEQ, SU, P], F16)
        s_pnT_l = sb("s_pnT_l", [DSEQ, SU, P], F16)
        s_on = sb("s_on", [P, SU, HD], F32)

        gq = sb("s_gq", [P, 1], F32)
        gq64 = sb("s_gq64", [P, 1], F32)
        psS = ps("s_psS", [P, 2, GQ, 2 * P], F32)
        psT = ps("s_psT", [P, KC, P], F32)
        psO = ps("s_psO", [P, NKV, P], F32)
        gq_ld, ck_ld, cv_ld, vn_ld, vnew_st, knew_st, sbias_ld, ssnk_ld = (
            sem("s_" + n) for n in ("gq_ld", "ck_ld", "cv_ld", "vn_ld", "vnew_st", "knew_st", "bias_ld", "snk_ld"))
        z_q, z_qh, z_ql, z_s, z_b, z_st, z_e, z_t, z_th, z_tl, z_o, z_on, z_ot, z_oh, z_ol, z_c = (
            sem("z_" + n) for n in ("q", "qh", "ql", "s", "b", "st", "e", "t", "th", "tl", "o", "on", "ot", "oh",
                                    "ol", "c"))
        block = c.enter_context(nc.Block())

        psS_f = psS[:].rearrange("p a r n -> p (a r n)")
        psS_q = psS_f[0:HD, 0:NH * TS].rearrange("d (h n) -> d h n", h=NH)
        psS_s = psS_f.rearrange("p (u n) -> p u n", u=SU)[:, :, 0:WIN + DSEQ]
        psS_t = psS_f[:, 0:SU * P].rearrange("p (u n) -> p u n", u=SU)
        psS_n = psS_f[:, SU * P:2 * SU * P].rearrange("p (u n) -> p u n", u=SU)
        psT_f = psT[:].rearrange("p k n -> p (k n)")
        psT_o = psT_f[:, 0:SU * HD].rearrange("p (u n) -> p u n", u=SU)
        psOT = psS_f[0:HD, 0:SU * P].rearrange("d (g h b r i) -> d g h b r i", g=NKV, h=2, b=4, r=GQ)

        def sample_oT(buf, grp, r):
            rows = slice((r % 2) * HD, (r % 2 + 1) * HD)
            return buf[rows, 2 * grp + r // 2, SEQ:SEQ + TS].rearrange("d (b i) -> d b i", i=DSEQ)

        def sample_oT_ps(grp, r):
            return psOT[:, grp, :, :, r, :].rearrange("d h b i -> d (h b) i")

        @block.sync
        def _(sp):
            sp.dma_start(gq[:], A["gq2"]).then_inc(gq_ld, 16)
            sp.dma_start(s_kT[:, :, 0:WIN], A["ckT"]).then_inc(ck_ld, 16)
            sp.dma_start(s_v[:], A["cvT"]).then_inc(cv_ld, 16)
            for b in range(NSEQ):
                r = slice(b * DSEQ, (b + 1) * DSEQ)
                sp.dma_start(s_vn[:, b, :], g.v_s[r, :]).then_inc(vn_ld, 16)
                sp.dma_start(A["ck_sample"][b, WIN - DSEQ:WIN, :], g.k_s[r, :]).then_inc(knew_st, 16)
                sp.dma_start(A["cv_sample"][b, WIN - DSEQ:WIN, :], g.v_s[r, :]).then_inc(vnew_st, 16)
            sp.wait_ge(knew_st, 16 * NSEQ)
            sp.wait_ge(vnew_st, 16 * NSEQ)

        @block.gpsimd
        def _(pool):
            for b4 in range(4):
                for r in range(GQ):
                    row = (b4 * GQ + r) * DSEQ
                    pool.dma_start(s_bias[row:row + DSEQ, :, :],
                                   bass.AP(tensor=A["dist_dram"].tensor, offset=r * RW + P - 1,
                                           ap=[[NH * RW - 1, DSEQ], [GQ * RW, NKV], [1, WIN + DSEQ]])).then_inc(sbias_ld, 16)
                    pool.dma_start(s_nsink[row:row + DSEQ, :],
                                   bass.AP(tensor=A["attn_sinks"].tensor, offset=r,
                                           ap=[[0, DSEQ], [GQ, NKV]]),
                                   allow_slow_non_contiguous=True).then_inc(ssnk_ld, 16)

        @block.scalar
        def _(act):
            act.wait_ge(z_c, 1)
            act.wait_ge(z_q, 1)
            for b in range(NSEQ):
                act.activation(s_qT_h[:, b], psS_q[:, :, b * DSEQ:(b + 1) * DSEQ], ACT.Copy,
                               scale=gq64[0:HD, 0:1]).then_inc(z_qh, 1)
            act.wait_ge(ck_ld, 16)
            act.wait_ge(z_c, 2)
            act.activation(s_kT_h[:], s_kT[:], ACT.Copy, scale=S_X).then_inc(z_qh, 1)
            act.wait_ge(cv_ld, 16)
            act.activation(s_v_h[:], s_v[:], ACT.Copy, scale=S_X).then_inc(z_qh, 1)
            act.wait_ge(vn_ld, 16 * NSEQ)
            act.activation(s_vn_h[:], s_vn[:], ACT.Copy, scale=S_X).then_inc(z_qh, 1)
            act.wait_ge(z_st, 2)
            for u in range(SU):
                act.activation(s_p[:, u], s_p[:, u], ACT.Exp, bias=s_st[:, 1, u:u + 1],
                               accum_out=s_st[:, 3, u:u + 1]).then_inc(z_e, 1)
            act.wait_ge(z_st, 3)
            act.activation(s_st[:, 4], s_st[:, 2], ACT.Exp).then_inc(z_e, 1)
            act.wait_ge(z_t, 2)
            act.activation(s_pT_h[:], psS_t[:], ACT.Copy, scale=S_X).then_inc(z_th, 1)
            act.activation(s_pnT_h[:], psS_n[0:DSEQ], ACT.Copy, scale=S_X).then_inc(z_th, 1)
            act.wait_ge(z_ot, 1)
            for grp in range(NKV):
                for r in range(GQ):
                    act.activation(sample_oT(g.oT_h, grp, r), sample_oT_ps(grp, r), ACT.Copy,
                                   scale=S_X).then_inc(z_oh, 1)

        @block.vector
        def _(dve):
            dve.wait_ge(gq_ld, 16)
            dve.tensor_scalar(gq64[:], gq[:], S_X, None, ALU.mult).then_inc(z_c, 1)
            dve.wait_ge(z_qh, NSEQ)
            for b in range(NSEQ):
                dve.scalar_tensor_tensor(s_qT_l[:, b], psS_q[:, :, b * DSEQ:(b + 1) * DSEQ], gq64[0:HD, 0:1],
                                         s_qT_h[:, b], op0=ALU.mult, op1=ALU.subtract).then_inc(z_ql, 1)
            dve.wait_ge(z_q, 2)
            dve.tensor_copy(s_kT[:, :, WIN:].rearrange("d (g b) i -> d g b i", g=NKV),
                            psO[0:HD, :, 0:TS].rearrange("d g (b i) -> d g b i", b=NSEQ)).then_inc(z_c, 1)
            dve.wait_ge(z_qh, NSEQ + 1)
            dve.scalar_tensor_tensor(s_kT_l[:], s_kT[:], S_X, s_kT_h[:], op0=ALU.mult,
                                     op1=ALU.subtract).then_inc(z_ql, 1)
            dve.wait_ge(z_qh, NSEQ + 3)
            dve.scalar_tensor_tensor(s_v_l[:], s_v[:], S_X, s_v_h[:], op0=ALU.mult,
                                     op1=ALU.subtract).then_inc(z_ql, 1)
            dve.scalar_tensor_tensor(s_vn_l[:], s_vn[:], S_X, s_vn_h[:], op0=ALU.mult,
                                     op1=ALU.subtract).then_inc(z_ql, 1)
            dve.wait_ge(ssnk_ld, 16 * 16)
            dve.wait_ge(sbias_ld, 16 * 16)
            dve.tensor_scalar(s_nsink[:], s_nsink[:], -1.0, None, ALU.mult).then_inc(z_b, 1)
            dve.wait_ge(z_s, 1)
            for half in range(2):
                dve.scalar_tensor_tensor(s_p[:, half::2], psS_s[:, half::2], 1.0 / (S_X * S_X * 8.0), s_bias[:],
                                         op0=ALU.mult, op1=ALU.add).then_inc(z_b, 1)
            dve.wait_ge(z_b, 3)
            dve.tensor_reduce(s_st[:, 0], s_p[:], AX.X, ALU.max).then_inc(z_st, 1)
            dve.wait_ge(z_st, 1)
            sink_b = s_nsink[:].unsqueeze(2).to_broadcast([P, NKV, 2])
            dve.scalar_tensor_tensor(s_st[:, 1].rearrange("p (g h) -> p g h", h=2),
                                     s_st[:, 0].rearrange("p (g h) -> p g h", h=2), -1.0, sink_b, op0=ALU.mult,
                                     op1=ALU.min).then_inc(z_st, 1)
            dve.wait_ge(z_st, 2)
            dve.tensor_tensor(s_st[:, 2].rearrange("p (g h) -> p g h", h=2),
                              s_st[:, 1].rearrange("p (g h) -> p g h", h=2), sink_b, ALU.subtract).then_inc(z_st, 1)
            dve.wait_ge(z_e, SU + 1)
            dve.tensor_tensor(s_st[:, 5], s_st[:, 3], s_st[:, 4], ALU.add).then_inc(z_st, 1)
            dve.wait_ge(z_st, 4)
            dve.reciprocal(s_st[:, 6], s_st[:, 5]).then_inc(z_st, 1)
            dve.wait_ge(z_th, 2)
            dve.scalar_tensor_tensor(s_pT_l[:], psS_t[:], S_X, s_pT_h[:], op0=ALU.mult,
                                     op1=ALU.subtract).then_inc(z_tl, 1)
            dve.scalar_tensor_tensor(s_pnT_l[:], psS_n[0:DSEQ], S_X, s_pnT_h[:], op0=ALU.mult,
                                     op1=ALU.subtract).then_inc(z_tl, 1)
            dve.wait_ge(z_o, 1)
            dve.wait_ge(z_st, 5)
            dve.scalar_tensor_tensor(s_on[:], psT_o, 1.0 / (S_X * S_X),
                                     s_st[:, 6].unsqueeze(2).to_broadcast([P, SU, HD]), op0=ALU.mult,
                                     op1=ALU.mult).then_inc(z_on, 1)
            dve.wait_ge(z_oh, NH)
            for grp in range(NKV):
                for r in range(GQ):
                    dve.scalar_tensor_tensor(sample_oT(g.oT_l, grp, r), sample_oT_ps(grp, r), S_X,
                                             sample_oT(g.oT_h, grp, r), op0=ALU.mult,
                                             op1=ALU.subtract).then_inc(z_ol, 1)

        @block.tensor
        def _(pe):
            for h in range(NH):
                last = pe.transpose(psS_q[:, h, :], g.q_s[0:TS, h * HD:(h + 1) * HD], g.ident[0:TS, 0:TS])
            last.then_inc(z_q, 1)
            for grp in range(NKV):
                last = pe.transpose(psO[0:HD, grp, 0:TS], g.k_s[0:TS, grp * HD:(grp + 1) * HD], g.ident[0:TS, 0:TS])
            last.then_inc(z_q, 1)
            pe.wait_ge(z_ql, NSEQ + 3)
            for grp in range(NKV):
                for b in range(NSEQ):
                    rows = slice(32 * (b % 4), 32 * (b % 4) + 32)
                    heads = slice(grp * GQ, (grp + 1) * GQ)
                    stat = tuple(q[:, b, heads].rearrange("d r i -> d (r i)") for q in (s_qT_h, s_qT_l))
                    last = mm3(pe, psS_s[rows, 2 * grp + b // 4, :], stat,
                               (s_kT_h[:, grp * NSEQ + b, :], s_kT_l[:, grp * NSEQ + b, :]), True, True)
            last.then_inc(z_s, 1)
            pe.wait_ge(z_b, 3)
            pe.wait_ge(z_e, SU)
            for u in range(SU):
                last = pe.transpose(psS_t[:, u, :], s_p[:, u, 0:WIN], g.ident[:])
            last.then_inc(z_t, 1)
            for u in range(SU):
                last = pe.transpose(psS_n[0:DSEQ, u, :], s_p[:, u, WIN:], g.ident[:])
            last.then_inc(z_t, 1)
            pe.wait_ge(z_tl, 2)
            for grp in range(NKV):
                for b in range(NSEQ):
                    rows = slice(32 * (b % 4), 32 * (b % 4) + 32)
                    u = 2 * grp + b // 4
                    cols = slice(grp * HD, (grp + 1) * HD)
                    mm3(pe, psT_o[rows, u, :], (s_pT_h[:, u, rows], s_pT_l[:, u, rows]),
                        (s_v_h[:, b, cols], s_v_l[:, b, cols]), True, False)
                    last = mm3(pe, psT_o[rows, u, :], (s_pnT_h[:, u, rows], s_pnT_l[:, u, rows]),
                               (s_vn_h[:, b, cols], s_vn_l[:, b, cols]), False, True)
            last.then_inc(z_o, 1)
            pe.wait_ge(z_on, 1)
            for u in range(SU):
                last = pe.transpose(psS_f[0:HD, u * P:(u + 1) * P], s_on[:, u, :], g.ident[:])
            last.then_inc(z_ot, 1)


def conv_phase(nc, sem, g, A):
    with ExitStack() as c:
        def sb(name, shape, dt):
            return c.enter_context(nc.sbuf_tensor(name, shape, dt))

        W32, WS = 3, 4
        w32 = sb("c_w32", [P, W32, D], F32)
        w_h = sb("c_w_h", [P, WS, KC, P], F16)
        w_l = sb("c_w_l", [P, WS, KC, P], F16)
        gate = sb("c_gate", [P, TM], F32)
        region = sb("c_region", [P, 6 * TM], F32)
        glu = region[:, 0:2 * GLU_W].rearrange("p (a n) -> p a n", a=2)
        th = region[:, 2 * GLU_W:2 * GLU_W + TM]
        a_s = region[:, 2 * GLU_W + TM:2 * GLU_W + 2 * TM]
        taps = sb("c_taps", [P, KC, TAPS], F32)
        vecs = sb("c_vecs", [P, 3, KC], F32)
        halves = sb("c_halves", [P, 2, KC], F32)
        ones = sb("c_ones", [P, P], F32)
        y = g.y
        work = region[:, 0:2 * TM].rearrange("p (a n) -> p a n", a=2)
        work2 = region[:, 2 * TM:4 * TM].rearrange("p (a n) -> p a n", a=2)
        rstd = region[:, 4 * TM:5 * TM]
        var = region[:, 5 * TM:6 * TM]
        psb = c.enter_context(nc.psum_tensor("c_psb", [P, 3, 512], F32))
        psa = c.enter_context(nc.psum_tensor("c_psa", [P, 3, 512], F32))

        w_ld, w_high, w_low, w_used = sem("c_w_ld"), sem("c_w_high"), sem("c_w_low"), sem("c_w_used")
        taps_ld, vec_ld, hist_ld, hist_st, setup = (
            sem("c_taps"), sem("c_vec"), sem("c_hist"), sem("c_hist_st"), sem("c_setup"))
        hist_ps = sem("c_hist_ps")
        b_done, a_done, th_done, a_out, glu_done, glu_free = (
            sem("c_b"), sem("c_a"), sem("c_th"), sem("c_aout"), sem("c_glu"), sem("c_glu_free"))
        tap_done = sem("c_tap")
        gate_mm, gate_out, gate_st = sem("c_gate_mm"), sem("c_gate_out"), sem("c_gate_st")
        mean_mm, cent, sqd, var_mm, v_done, sq_root, r_done = (
            sem("c_mean"), sem("c_cent"), sem("c_sqd"), sem("c_var"), sem("c_v"), sem("c_root"), sem("c_r"))
        z_done, zt, zi, u_done, hi_done, lo_done = (
            sem("c_z"), sem("c_zt"), sem("c_zi"), sem("c_u"), sem("c_hi"), sem("c_lo"))
        block = c.enter_context(nc.Block())
        NTAP = 2 * TAPS

        def slot(buf, n):
            if isinstance(n, int):
                return buf[:, n % 2]
            return buf[:, ds(n % 2, 1)].rearrange("p a n -> p (a n)")

        def slot3(buf, n):
            return buf[:, ds(n % WS, 1)].rearrange("p a k n -> p (a k) n")

        def slot32(n):
            return w32[:, ds(n % W32, 1)].rearrange("p a n -> p (a n)")

        banks = (psa, psb)

        def thirds(buf):
            return buf.rearrange("p (s n) -> p s n", s=3)

        def row(buf, k):
            return buf[:, ds(k, 1), :].rearrange("p a n -> p (a n)")

        @block.sync
        def _(sp):
            sp.dma_start(taps[:], A["tapsT"]).then_inc(taps_ld, 16)
            sp.dma_start(vecs[:], A["conv_vecs"]).then_inc(vec_ld, 16)
            with sp.Fori(0, 4 * KC) as n:
                sp.wait_ge(w_ld, 16 * n)
                sp.wait_ge(w_low, n)
                sp.dma_start(slot32(n), A["w_feat"][ds(n, 1)].rearrange("a p n -> (a p) n")).then_inc(w_ld, 16)

        @block.gpsimd
        def _(pool):
            pool.wait_ge(setup, 1)
            with pool.Fori(0, KC) as k:
                pool.wait_ge(hist_ld, 16 * k)
                pool.wait_ge(glu_free, k + 1)
                pool.wait_ge(hist_st, 16 * k)
                pool.wait_ge(hist_ps, 16 * k)
                pool.dma_start(glu[:, ds(k % 2, 1), HIST + SEQ:].rearrange("p a (b n) -> p (a b) n", b=NSEQ)[:, :, 0:HIST],
                               A["stateT"][ds(k * P, P)]).then_inc(hist_ld, 16)
                pool.wait_ge(glu_done, 2 * k + 2)
                pool.dma_start(A["sc_prompt"][ds(k * P, P), :],
                               glu[:, ds(k % 2, 1), SEQ:SEQ + HIST].rearrange("p a n -> p (a n)")).then_inc(hist_ps, 16)
                pool.dma_start(A["sc_sample"][ds(k * P, P)],
                               glu[:, ds(k % 2, 1), HIST + SEQ:].rearrange("p a (b n) -> p (a b) n", b=NSEQ)
                               [:, :, DSEQ:]).then_inc(hist_st, 16)
            pool.wait_ge(hist_st, 16 * KC)
            pool.wait_ge(hist_ps, 16 * KC)

        @block.scalar
        def _(act):
            def cut(n):
                act.wait_ge(w_ld, 16 * n + 16)
                act.wait_ge(w_used, n + 1)
                act.activation(slot3(w_h, n), slot32(n).rearrange("p (k m) -> p k m", k=KC), ACT.Copy,
                               scale=S_W).then_inc(w_high, 1)

            def glu_parts(k):
                act.wait_ge(b_done, k + 1)
                act.wait_ge(glu_done, 2 * k)
                act.activation(thirds(th), psb[:, :, 0:THIRD], ACT.Tanh, scale=0.5 * UNSCALE).then_inc(th_done, 1)
                act.wait_ge(a_done, k + 1)
                act.activation(thirds(a_s), psa[:, :, 0:THIRD], ACT.Copy, scale=0.5 * UNSCALE).then_inc(a_out, 1)

            def gate_leaves(i, bank):
                act.wait_ge(gate_mm, i + 1)
                act.wait_ge(gate_st, 16 * i)
                act.activation(thirds(gate[:]), bank[:, :, 0:THIRD], ACT.Tanh, scale=0.5 * UNSCALE).then_inc(gate_out, 1)
                act.wait_ge(gate_out, i + 1)
                act.dma_start(A["gates"][ds(i, 1)].rearrange("a p n -> (a p) n"), gate[:]).then_inc(gate_st, 16)

            for n in range(3):
                cut(n)
            glu_parts(0)
            with act.Fori(1, KC) as k:
                for i in range(3):
                    cut(3 * k + i)
                gate_leaves(k - 1, psb)
                glu_parts(k)
            for n in range(3 * KC, 3 * KC + 3):
                cut(n)
            gate_leaves(KC - 1, psb)
            for i in range(3):
                cut(3 * KC + 3 + i)
                gate_leaves(KC + i, banks[i % 2])
            cut(4 * KC - 2)
            act.wait_ge(hist_st, 16 * KC)
            act.wait_ge(hist_ps, 16 * KC)
            with act.Fori(0, KC) as k:
                act.wait_ge(cent, k + 1)
                act.wait_ge(var_mm, k // 2 * 2)
                act.activation(slot(work, k), row(y, k), ACT.Square).then_inc(sqd, 1)
            cut(4 * KC - 1)
            gate_leaves(KC + 3, psa)
            act.wait_ge(v_done, 1)
            act.activation(rstd, var, ACT.Sqrt).then_inc(sq_root, 1)

            def swish(k):
                act.wait_ge(z_done, k + 1)
                act.activation(slot(work, k), row(y, k), ACT.Tanh, scale=halves[:, 0, ds(k, 1)],
                               bias=halves[:, 1, ds(k, 1)]).then_inc(zt, 1)
                act.activation(slot(work2, k), row(y, k), ACT.Identity, scale=vecs[:, 1, ds(k, 1)],
                               bias=vecs[:, 2, ds(k, 1)]).then_inc(zi, 1)
                act.wait_ge(u_done, k + 1)
                act.activation(row(g.caT_h, k), row(y, k), ACT.Copy, scale=0.5 * S_X).then_inc(hi_done, 1)

            with act.Fori(0, 2) as j:
                for i in range(2):
                    swish(4 * j + 2 * i)
                    swish(4 * j + 2 * i + 1)
                    gate_leaves(KC + 4 + 2 * j + i, banks[i])
            act.wait_ge(gate_st, 16 * 2 * KC)

        @block.vector
        def _(dve):
            dve.memset(glu[:, :, 0:HIST], 0.0).then_inc(setup, 1)
            dve.memset(y[:, :, T:TM], 0.0).then_inc(setup, 1)
            dve.memset(ones[:], 1.0 / D).then_inc(setup, 1)
            dve.sem_inc(w_used, WS)
            dve.sem_inc(w_low, W32 - 1)
            dve.sem_inc(glu_free, 2)
            dve.wait_ge(vec_ld, 16)
            dve.tensor_scalar(halves[:], vecs[:, 1:3], 0.5, None, ALU.mult).then_inc(setup, 1)
            dve.wait_ge(taps_ld, 16)
            dve.wait_ge(setup, 4)

            def low(n):
                dve.wait_ge(w_high, n + 1)
                dve.scalar_tensor_tensor(slot3(w_l, n), slot32(n).rearrange("p (k m) -> p k m", k=KC), S_W,
                                         slot3(w_h, n), op0=ALU.mult, op1=ALU.subtract).then_inc(w_low, 1)

            def chunk(k):
                dve.wait_ge(th_done, k + 1)
                dve.wait_ge(a_out, k + 1)
                dve.wait_ge(hist_ld, 16 * k + 16)
                dve.scalar_tensor_tensor(slot(glu, k)[:, HIST:HIST + SEQ], th[:, 0:SEQ], 1.0, a_s[:, 0:SEQ],
                                         op0=ALU.add, op1=ALU.mult).then_inc(glu_done, 1)
                seqs = slot(glu, k)[:, HIST + SEQ:].rearrange("p (b n) -> p b n", b=NSEQ)
                dve.scalar_tensor_tensor(seqs[:, :, HIST:], th[:, SEQ:T].rearrange("p (b i) -> p b i", b=NSEQ), 1.0,
                                         a_s[:, SEQ:T].rearrange("p (b i) -> p b i", b=NSEQ),
                                         op0=ALU.add, op1=ALU.mult).then_inc(glu_done, 1)

            def conv(k):
                seqs = slot(glu, k)[:, HIST + SEQ:].rearrange("p (b n) -> p b n", b=NSEQ)
                y_p = row(y, k)[:, 0:SEQ]
                y_s = row(y, k)[:, SEQ:T].rearrange("p (b i) -> p b i", b=NSEQ)
                dve.wait_ge(glu_done, 2 * k + 2)
                dve.tensor_scalar(y_p, slot(glu, k)[:, 0:SEQ], taps[:, ds(k, 1), 0:1].rearrange("p a b -> p (a b)"),
                                  vecs[:, 0, ds(k, 1)], ALU.mult, ALU.add).then_inc(tap_done, 1)
                dve.tensor_scalar(y_s, seqs[:, :, 0:DSEQ], taps[:, ds(k, 1), 0:1].rearrange("p a b -> p (a b)"),
                                  vecs[:, 0, ds(k, 1)], ALU.mult, ALU.add).then_inc(tap_done, 1)
                for j in range(1, TAPS):
                    tap = taps[:, ds(k, 1), j:j + 1].rearrange("p a b -> p (a b)")
                    dve.wait_ge(tap_done, NTAP * k + 2 * j - 1)
                    dve.scalar_tensor_tensor(y_p, slot(glu, k)[:, j:j + SEQ], tap, y_p, op0=ALU.mult,
                                             op1=ALU.add).then_inc(tap_done, 1)
                    dve.wait_ge(tap_done, NTAP * k + 2 * j)
                    last = dve.scalar_tensor_tensor(y_s, seqs[:, :, j:j + DSEQ], tap, y_s, op0=ALU.mult,
                                                    op1=ALU.add)
                    last.then_inc(tap_done, 1)
                dve.wait_ge(tap_done, NTAP * k + NTAP)
                dve.sem_inc(glu_free, 1)

            for n in range(3):
                low(n)
            with dve.Fori(0, KC - 1) as k:
                chunk(k)
                for i in range(3):
                    low(3 * k + 3 + i)
                conv(k)
            chunk(KC - 1)
            for n in range(3 * KC, 3 * KC + 3):
                low(n)
            conv(KC - 1)
            for n in range(3 * KC + 3, 4 * KC - 1):
                low(n)
            dve.wait_ge(mean_mm, 1)
            with dve.Fori(0, KC) as k:
                dve.tensor_tensor(thirds(row(y, k)), thirds(row(y, k)), psb[:, :, 0:THIRD],
                                  ALU.subtract).then_inc(cent, 1)
            low(4 * KC - 1)
            dve.wait_ge(var_mm, KC)
            dve.tensor_scalar(thirds(var), psb[:, :, 0:THIRD], EPS, None, ALU.add).then_inc(v_done, 1)
            dve.wait_ge(sq_root, 1)
            dve.reciprocal(rstd, rstd).then_inc(r_done, 1)
            dve.wait_ge(r_done, 1)
            dve.tensor_tensor(var, var, rstd, ALU.mult).then_inc(r_done, 1)
            dve.wait_ge(r_done, 2)
            dve.tensor_tensor(var, var, rstd, ALU.mult).then_inc(r_done, 1)
            dve.wait_ge(r_done, 3)
            dve.tensor_scalar(var, var, -0.5, 1.5, ALU.mult, ALU.add).then_inc(r_done, 1)
            dve.wait_ge(r_done, 4)
            dve.tensor_tensor(rstd, rstd, var, ALU.mult).then_inc(r_done, 1)
            dve.wait_ge(r_done, 5)

            def swish_low(k):
                dve.wait_ge(zi, k + 1)
                dve.wait_ge(zt, k + 1)
                dve.scalar_tensor_tensor(row(y, k), slot(work, k), 1.0, slot(work2, k), op0=ALU.add,
                                         op1=ALU.mult).then_inc(u_done, 1)
                dve.wait_ge(hi_done, k + 1)
                dve.scalar_tensor_tensor(row(g.caT_l, k), row(y, k), 0.5 * S_X, row(g.caT_h, k), op0=ALU.mult,
                                         op1=ALU.subtract).then_inc(lo_done, 1)

            def scale(k):
                dve.tensor_tensor(row(y, k), row(y, k), rstd, ALU.mult).then_inc(z_done, 1)

            dve.wait_ge(sqd, KC)
            scale(0)
            with dve.Fori(1, KC) as k:
                scale(k)
                swish_low(k - 1)
            swish_low(KC - 1)

        @block.tensor
        def _(pe):
            def product(n, out, done):
                pe.wait_ge(w_low, n + W32)
                for s in range(3):
                    cols = slice(s * THIRD, (s + 1) * THIRD)
                    for k in range(KC):
                        last = mm3(pe, out[:, s, 0:THIRD], (slot3(w_h, n)[:, k], slot3(w_l, n)[:, k]),
                                   (g.xnT_h[:, k, cols], g.xnT_l[:, k, cols]), k == 0, k == KC - 1)
                last.then_inc(done, 1)
                return last

            def used(done, count):
                pe.wait_ge(done, count)
                pe.sem_inc(w_used, 1)

            with pe.Fori(0, KC) as k:
                pe.wait_ge(gate_out, k)
                product(3 * k, psb, b_done)
                used(b_done, k + 1)
                pe.wait_ge(a_out, k)
                product(3 * k + 1, psa, a_done)
                used(a_done, k + 1)
                pe.wait_ge(th_done, k + 1)
                product(3 * k + 2, psb, gate_mm)
                used(gate_mm, k + 1)

            def gate_b(i):
                product(3 * KC + i, banks[i % 2], gate_mm)
                used(gate_mm, KC + i + 1)

            pe.wait_ge(a_out, KC)
            gate_b(0)
            pe.wait_ge(gate_out, KC)
            gate_b(1)
            pe.wait_ge(gate_out, KC + 1)
            gate_b(2)
            pe.wait_ge(gate_out, KC + 2)
            pe.wait_ge(tap_done, NTAP * KC)
            for k in range(KC):
                for s in range(3):
                    last = pe.matmul(psb[:, s, 0:THIRD], ones[:], y[:, k, s * THIRD:(s + 1) * THIRD], start=k == 0,
                                     stop=k == KC - 1)
            last.then_inc(mean_mm, 1)
            pe.wait_ge(gate_out, KC + 3)
            product(3 * KC + 3, psa, gate_mm)
            used(gate_mm, KC + 4)
            pe.wait_ge(cent, KC)
            for k in range(KC):
                pe.wait_ge(sqd, k + 1)
                for s in range(3):
                    last = pe.matmul(psb[:, s, 0:THIRD], ones[:], work[:, k % 2, s * THIRD:(s + 1) * THIRD],
                                     start=k == 0, stop=k == KC - 1)
                last.then_inc(var_mm, 1)
            pe.wait_ge(gate_out, KC + 4)
            gate_b(4)
            pe.wait_ge(v_done, 1)
            gate_b(5)
            pe.wait_ge(gate_out, KC + 5)
            gate_b(6)
            pe.wait_ge(gate_out, KC + 6)
            gate_b(7)


def merge_phase(nc, sem, g, A):
    with ExitStack() as c:
        def sb(name, shape, dt):
            return c.enter_context(nc.sbuf_tensor(name, shape, dt))

        NM = 2
        w32 = sb("m_w32", [P, 2, D], F32)
        w_h = sb("m_w_h", [P, 2 * NM, KC, P], F16)
        w_l = sb("m_w_l", [P, 2 * NM, KC, P], F16)
        bias = sb("m_bias", [P, KC], F32)
        conv = sb("m_conv", [P, 2, THIRD], F32)
        gates = sb("m_gates", [P, 2, 2, TM], F32)
        u = sb("m_u", [P, 2, THIRD], F32)
        v = sb("m_v", [P, 2, THIRD], F32)
        m = sb("m_m", [P, 2, THIRD], F32)
        psum = c.enter_context(nc.psum_tensor("m_ps", [P, 2 * NM, 512], F32))
        g_ld, g_used = sem("m_g_ld"), sem("m_g_used")
        w_ld, w_high, w_low, w_used, b_ld = (
            sem("m_w_ld"), sem("m_w_high"), sem("m_w_low"), sem("m_w_used"), sem("m_b_ld"))
        mm, out_a, v_done, u_done, m_done, hi, lo = (
            sem("m_mm"), sem("m_out"), sem("m_v"), sem("m_u"), sem("m_m"), sem("m_hi"), sem("m_lo"))
        block = c.enter_context(nc.Block())

        def slot(buf, n):
            return buf[:, ds(n % 2, 1)].rearrange("p a n -> p (a n)")

        def bank(n, i):
            return psum[:, ds((n % 2) * NM + i, 1), 0:THIRD].rearrange("p a n -> p (a n)")

        def gate_cols(j, i, s):
            return gates[:, ds(j % 2, 1), i, s * THIRD:(s + 1) * THIRD].rearrange("p a n -> p (a n)")

        def cols(buf, k, s):
            return buf[:, ds(k, 1), ds(s * THIRD, THIRD)].rearrange("p a n -> p (a n)")

        @block.sync
        def _(sp):
            sp.dma_start(bias[:], A["b_conv_outT"]).then_inc(b_ld, 16)
            with sp.Fori(0, NM * KC) as n:
                sp.wait_ge(w_ld, 16 * n)
                sp.wait_ge(w_low, n // 2 * 2)
                sp.dma_start(slot(w32, n), A["w_feat"][ds(n + 4 * KC, 1)].rearrange("a p n -> (a p) n")).then_inc(w_ld, 16)

        @block.gpsimd
        def _(pool):
            by_chunk = A["gates"].rearrange("(i j) p n -> j p i n", i=2)
            with pool.Fori(0, KC) as j:
                pool.wait_ge(g_ld, 16 * j)
                pool.wait_ge(g_used, j + 1)
                pool.dma_start(gates[:, ds(j % 2, 1)].rearrange("p a i n -> p (a i) n"),
                               by_chunk[ds(j, 1)].rearrange("a p i n -> (a p) i n")).then_inc(g_ld, 16)

        def weights(buf, n):
            return buf[:, ds(n % (2 * NM), 1)].rearrange("p a k m -> p (a k) m")

        @block.scalar
        def _(act):
            act.wait_ge(b_ld, 16)

            def cut(j):
                act.wait_ge(w_used, j + 1)
                for i in range(NM):
                    n = j * NM + i
                    act.wait_ge(w_ld, 16 * n + 16)
                    act.activation(weights(w_h, n), slot(w32, n).rearrange("p (k m) -> p k m", k=KC), ACT.Copy,
                                   scale=S_W).then_inc(w_high, 1)

            def step(j, s):
                n = 3 * j + s
                act.wait_ge(mm, n + 1)
                act.activation(slot(conv, n), bank(n, 0), ACT.Identity, scale=UNSCALE,
                               bias=bias[:, ds(j, 1)]).then_inc(out_a, 1)
                act.wait_ge(m_done, n + 1)
                act.activation(cols(g.mT_h, j, s), slot(m, n), ACT.Copy, scale=0.5 * S_X).then_inc(hi, 1)

            cut(0)
            with act.Fori(0, KC - 1) as j:
                cut(j + 1)
                for s in range(3):
                    step(j, s)
            for s in range(3):
                step(KC - 1, s)

        @block.vector
        def _(dve):
            dve.memset(g.mT_h[:, :, TM:TP], 0.0).then_inc(lo, 1)
            dve.memset(g.mT_l[:, :, TM:TP], 0.0).then_inc(lo, 1)
            dve.sem_inc(v_done, 1)
            dve.sem_inc(w_used, 2)
            dve.sem_inc(g_used, 2)

            def low(j):
                for i in range(NM):
                    n = j * NM + i
                    dve.wait_ge(w_high, n + 1)
                    dve.scalar_tensor_tensor(weights(w_l, n), slot(w32, n).rearrange("p (k m) -> p k m", k=KC), S_W,
                                             weights(w_h, n), op0=ALU.mult, op1=ALU.subtract).then_inc(w_low, 1)

            def step(j, s):
                n = 3 * j + s
                dve.wait_ge(out_a, n + 1)
                dve.wait_ge(g_ld, 16 * j + 16)
                dve.scalar_tensor_tensor(slot(v, n), gate_cols(j, 1, s), 1.0, bank(n, 1), op0=ALU.add,
                                         op1=ALU.mult).then_inc(v_done, 1)
                dve.scalar_tensor_tensor(slot(u, n), gate_cols(j, 0, s), 1.0, slot(conv, n), op0=ALU.add,
                                         op1=ALU.mult).then_inc(u_done, 1)
                dve.wait_ge(v_done, n + 2)
                dve.wait_ge(u_done, n + 1)
                dve.scalar_tensor_tensor(slot(m, n), slot(v, n), UNSCALE, slot(u, n), op0=ALU.mult,
                                         op1=ALU.add).then_inc(m_done, 1)
                dve.wait_ge(hi, n + 1)
                dve.scalar_tensor_tensor(cols(g.mT_l, j, s), slot(m, n), 0.5 * S_X, cols(g.mT_h, j, s),
                                         op0=ALU.mult, op1=ALU.subtract).then_inc(lo, 1)

            low(0)
            with dve.Fori(0, KC - 1) as j:
                low(j + 1)
                for s in range(3):
                    step(j, s)
                dve.wait_ge(m_done, 3 * j + 3)
                dve.sem_inc(g_used, 1)
            for s in range(3):
                step(KC - 1, s)

        @block.tensor
        def _(pe):
            movs = ((g.caT_h, g.caT_l), (g.oT_h, g.oT_l))
            with pe.Fori(0, KC) as j:
                with pe.Fori(0, 3) as s:
                    pe.wait_ge(w_low, NM * j + NM)
                    n = 3 * j + s
                    pe.wait_ge(v_done, n)
                    for i, (high, low) in enumerate(movs):
                        for k in range(KC):
                            last = mm3(pe, bank(n, i), (weights(w_h, NM * j + i)[:, k], weights(w_l, NM * j + i)[:, k]),
                                       (high[:, k, ds(s * THIRD, THIRD)], low[:, k, ds(s * THIRD, THIRD)]),
                                       k == 0, k == KC - 1)
                    last.then_inc(mm, 1)
                pe.wait_ge(mm, 3 * j + 3)
                pe.sem_inc(w_used, 1)


def out_phase(nc, sem, g, A):
    with ExitStack() as c:
        def sb(name, shape, dt):
            return c.enter_context(nc.sbuf_tensor(name, shape, dt))

        w32 = sb("o_w32", [P, 2, D], F32)
        w_h = sb("o_w_h", [P, KC, D], F16)
        w_l = sb("o_w_l", [P, KC, D], F16)
        r32 = sb("o_r32", [P, KC, RT], F32)
        r_h = sb("o_r_h", [P, KC, RT], F16)
        r_l = sb("o_r_l", [P, KC, RT], F16)
        rb = sb("o_rb", [P, RT], F32)
        gain = sb("o_gain", [P, D], F32)
        x_in = sb("o_x", [P, 2, D], F32)
        junk = sb("o_junk", [P, D], F32)
        hn = sb("o_hn", [P, 2, D], F32)
        hnT_h = sb("o_hnT_h", [P, KC, P], F16)
        hnT_l = sb("o_hnT_l", [P, KC, P], F16)
        ss = sb("o_ss", [P, 1], F32)
        ms = sb("o_ms", [P, 1], F32)
        rstd = sb("o_rstd", [P, 1], F32)
        psH = c.enter_context(nc.psum_tensor("o_psH", [P, 2, D], F32))
        psT = c.enter_context(nc.psum_tensor("o_psT", [P, KC, P], F32))
        psL = c.enter_context(nc.psum_tensor("o_psL", [P, RT], F32))
        w_ld, w_high, w_low, r_ld, rb_ld, gain_ld, x_ld = (
            sem("o_" + n) for n in ("w_ld", "w_high", "w_low", "r_ld", "rb_ld", "gain_ld", "x_ld"))
        mm, h_done, sum_done, mean_done, rstd_done, hn_done, hn_st = (
            sem("o_" + n) for n in ("mm", "h", "sum", "mean", "rstd", "hn", "hn_st"))
        T_done, T_high, T_low, l_mm, l_done, r_cut = (
            sem("o_" + n) for n in ("T", "T_high", "T_low", "l_mm", "l", "r_cut"))
        block = c.enter_context(nc.Block())

        def slot(buf, n):
            if isinstance(n, int):
                return buf[:, n % 2]
            return buf[:, ds(n % 2, 1)].rearrange("p a n -> p (a n)")

        def row(buf, k):
            return buf[:, ds(k, 1), :].rearrange("p a n -> p (a n)")

        @block.sync
        def _(sp):
            sp.dma_start(r32[:], A["w_rt"]).then_inc(r_ld, 16)
            sp.dma_start(gain[:], rows_on_partitions(A["norm_ffn_g"], P, D)).then_inc(gain_ld, 16)
            sp.dma_start(rb[:], rows_on_partitions(A["b_rt"], P, RT)).then_inc(rb_ld, 16)
            with sp.Fori(0, KC) as k:
                sp.wait_ge(w_ld, 16 * k)
                sp.wait_ge(w_low, k // 2 * 2)
                sp.dma_start(slot(w32, k), A["w_out"][ds(k * P, P), :]).then_inc(w_ld, 16)
            with sp.Fori(0, TT) as t:
                sp.wait_ge(x_ld, 16 * t)
                sp.wait_ge(h_done, t // 2 * 2)
                sp.dma_start(slot(x_in, t), A["x_all"][ds(t * P, P), :]).then_inc(x_ld, 16)

        @block.scalar
        def _(act):
            act.wait_ge(r_ld, 16)
            act.activation(r_h[:], r32[:], ACT.Copy, scale=S_W).then_inc(r_cut, 1)
            with act.Fori(0, KC) as k:
                act.wait_ge(w_ld, 16 * k + 16)
                act.activation(row(w_h, k), slot(w32, k), ACT.Copy, scale=S_W).then_inc(w_high, 1)
            with act.Fori(0, TT) as t:
                act.wait_ge(h_done, t + 1)
                act.wait_ge(mean_done, t)
                act.activation(junk[:], row(g.h, t), ACT.Square, accum_out=ss[:]).then_inc(sum_done, 1)
                act.wait_ge(T_done, t + 1)
                act.wait_ge(l_mm, t)
                act.activation(hnT_h[:], psT[:], ACT.Copy, scale=S_X).then_inc(T_high, 1)

        @block.gpsimd
        def _(pool):
            with pool.Fori(0, TT) as t:
                pool.wait_ge(mean_done, t + 1)
                pool.wait_ge(hn_done, t)
                pool.tensor_tensor(rstd[:], ms[:], g.neg_half[:, 0:1], ALU.pow).then_inc(rstd_done, 1)
                pool.wait_ge(hn_done, t + 1)
                pool.wait_ge(hn_st, 16 * t)
                pool.dma_start(A["hn_dram"].rearrange("(k r) d -> r k d", k=2)[ds(t * P, P)],
                               slot(hn, t).unsqueeze(1).to_broadcast([P, 2, D])).then_inc(hn_st, 16)
            pool.wait_ge(hn_st, 16 * TT)

        @block.vector
        def _(dve):
            dve.wait_ge(r_cut, 1)
            dve.scalar_tensor_tensor(r_l[:], r32[:], S_W, r_h[:], op0=ALU.mult, op1=ALU.subtract).then_inc(r_cut, 1)
            with dve.Fori(0, KC) as k:
                dve.wait_ge(w_high, k + 1)
                dve.scalar_tensor_tensor(row(w_l, k), slot(w32, k), S_W, row(w_h, k), op0=ALU.mult,
                                         op1=ALU.subtract).then_inc(w_low, 1)
            dve.wait_ge(gain_ld, 16)
            dve.wait_ge(rb_ld, 16)

            def residual(t):
                dve.wait_ge(mm, t + 1)
                dve.wait_ge(x_ld, 16 * t + 16)
                dve.scalar_tensor_tensor(row(g.h, t), slot(psH, t), UNSCALE, slot(x_in, t), op0=ALU.mult,
                                         op1=ALU.add).then_inc(h_done, 1)
                dve.wait_ge(sum_done, t + 1)
                dve.tensor_scalar(ms[:], ss[:], 1.0 / D, EPS, ALU.mult, ALU.add).then_inc(mean_done, 1)
                dve.wait_ge(rstd_done, t + 1)
                dve.wait_ge(hn_st, 16 * (t // 2 * 2))
                dve.scalar_tensor_tensor(slot(hn, t), row(g.h, t), rstd[:, 0:1], gain[:], op0=ALU.mult,
                                         op1=ALU.mult).then_inc(hn_done, 1)

            def low(t):
                dve.wait_ge(T_high, t + 1)
                dve.scalar_tensor_tensor(hnT_l[:], psT[:], S_X, hnT_h[:], op0=ALU.mult,
                                         op1=ALU.subtract).then_inc(T_low, 1)

            def logits(t):
                dve.wait_ge(l_mm, t + 1)
                dve.scalar_tensor_tensor(row(g.logits, t), psL[:], UNSCALE, rb[:], op0=ALU.mult,
                                         op1=ALU.add).then_inc(l_done, 1)

            residual(0)
            with dve.Fori(1, TT) as t:
                low(t - 1)
                residual(t)
                logits(t - 1)
            low(TT - 1)
            logits(TT - 1)

        @block.tensor
        def _(pe):
            pe.wait_ge(w_low, KC)

            def half(t, nb):
                cols = slice(nb * 512, (nb + 1) * 512)
                for k in range(KC):
                    last = mm3(pe, slot(psH, t)[:, cols], (g.mT_h[:, k, ds(t * P, P)], g.mT_l[:, k, ds(t * P, P)]),
                               (w_h[:, k, cols], w_l[:, k, cols]), k == 0, k == KC - 1)
                if nb:
                    last.then_inc(mm, 1)

            def turn(t):
                pe.wait_ge(hn_done, t + 1)
                for k in range(KC):
                    last = pe.transpose(psT[:, k, :], hn[:, t_par(t), k * P:(k + 1) * P], g.ident[:])
                last.then_inc(T_done, 1)

            par = [0]

            def t_par(t):
                return par[0]

            def route(t):
                pe.wait_ge(T_low, t + 1)
                pe.wait_ge(l_done, t)
                for k in range(KC):
                    last = mm3(pe, psL[:], (hnT_h[:, k, :], hnT_l[:, k, :]), (r_h[:, k, :], r_l[:, k, :]), k == 0,
                               k == KC - 1)
                last.then_inc(l_mm, 1)

            def tile(t, p_prev):
                par[0] = p_prev
                pe.wait_ge(h_done, (t - 1) if not isinstance(t, int) else max(t - 1, 0))
                half(t, 0)
                turn(t - 1)
                half(t, 1)
                route(t - 1)

            half(0, 0)
            half(0, 1)
            pe.wait_ge(r_cut, 2)
            with pe.Fori(0, TT // 2) as u:
                tile(2 * u + 1, 0)
                tile(2 * u + 2, 1)
            par[0] = (TT - 1) % 2
            turn(TT - 1)
            route(TT - 1)


def route_phase(nc, sem, g, A):
    with ExitStack() as c:
        def sb(name, shape, dt):
            return c.enter_context(nc.sbuf_tensor(name, shape, dt))

        iota = sb("r_iota", [P, NBLK], F32)
        upper = sb("r_upper", [P, P], F32)
        ones = sb("r_ones", [P, P], F32)
        gpad = sb("r_gpad", [P, TT, 8], F32)
        gmx = sb("r_gmx", [P, TT, 8], F32)
        gix = sb("r_gix", [P, TT, 8], U32)
        gi = sb("r_gi", [P, TT], F32)
        goh = sb("r_goh", [P, TT, NG], F32)
        gex = sb("r_gex", [P, TT, NG], F32)
        pg = sb("r_pg", [P, 2, TT], F32)
        em = sb("r_em", [P, TT, NG, EPG], F32)
        es = sb("r_es", [P, TT, EPG], F32)
        emx = sb("r_emx", [P, TT, 8], F32)
        eix = sb("r_eix", [P, TT, 8], U32)
        eid = sb("r_eid", [P, 2, TT], F32)
        tmp = sb("r_tmp", [P, 4, TT], F32)
        oh = sb("r_oh", [P, 2, TT, NE], F32)
        both = sb("r_both", [P, TT, NE], F32)
        pre = sb("r_pre", [P, TT + 1, NE], F32)
        cnt = sb("r_cnt", [P, 4, NE], F32)
        cnt_i = sb("r_cnt_i", [P, 2, NE], I32)
        rank = sb("r_rank", [P, TT, NE], F32)
        picked = sb("r_picked", [P, 2, TT, NE], F32)
        dest_f = sb("r_dest_f", [P, 2, TT], F32)
        cmp = sb("r_cmp", [1, NBLK, NE], F32)
        ctl_f = sb("r_ctl_f", [1, NBLK + 1], F32)
        pair = sb("r_pair", [P, 2, TT], U32)
        unused = sb("r_unused", [P, NBLK + 1], U32)
        psR = c.enter_context(nc.psum_tensor("r_psR", [P, TT * NE], F32))
        psC = c.enter_context(nc.psum_tensor("r_psC", [P, TT * NE], F32))
        iota_ld, upper_ld, unused_st, scat = sem("r_iota_ld"), sem("r_upper_ld"), sem("r_unused_st"), sem("r_scat")
        ready, step, gexp, eexp, rank_mm, dest_done, toks = (
            sem("r_" + n) for n in ("ready", "step", "gexp", "eexp", "rank_mm", "dest", "toks"))
        block = c.enter_context(nc.Block())
        steps = []

        @block.sync
        def _(sp):
            sp.dma_start(iota[:], A["c_iota"]).then_inc(iota_ld, 16)
            sp.dma_start(upper[:], A["c_upper"]).then_inc(upper_ld, 16)
            sp.wait_ge(ready, 1)
            sp.dma_start(A["pair_dram"].rearrange("(p n) a -> p (n a)", p=P), unused[:]).then_inc(unused_st, 16)

        @block.gpsimd
        def _(pool):
            pool.iota(pair[:], [[TP, 2], [P, TT]], base=0, channel_multiplier=1).then_inc(toks, 1)
            pool.wait_ge(toks, 1)
            pool.wait_ge(unused_st, 16)
            pool.wait_ge(dest_done, 1)
            for k in range(2):
                for t in range(TT):
                    rows = P if t < NT else TS
                    pool.indirect_dma_start(out=A["pair_dram"],
                                            out_offset=bass.IndirectOffsetOnAxis(ap=g.dest[0:rows, k, t:t + 1], axis=0),
                                            in_=pair[0:rows, k, t:t + 1], in_offset=None).then_inc(scat, 16)
            pool.wait_ge(scat, 16 * 2 * TT)

        @block.scalar
        def _(act):
            act.wait_ge(gexp, 1)
            act.activation(gex[:], gex[:], ACT.Exp).then_inc(gexp, 1)
            act.wait_ge(eexp, 1)
            act.activation(tmp[:, 1], tmp[:, 0], ACT.Exp).then_inc(eexp, 1)

        @block.tensor
        def _(pe):
            pe.wait_ge(rank_mm, 1)
            pe.wait_ge(upper_ld, 16)
            flat = both[:].rearrange("p t e -> p (t e)")
            pe.matmul(psR[:], upper[:], flat, start=True, stop=True)
            pe.matmul(psC[:], ones[:], flat, start=True, stop=True).then_inc(rank_mm, 1)

        @block.vector
        def _(dve):
            def done(ins):
                steps.append(1)
                ins.then_inc(step, 1)
                dve.wait_ge(step, len(steps))

            def over_e(ap):
                return ap.unsqueeze(2).to_broadcast([P, TT, NE])

            dve.memset(unused[:], T).then_inc(ready, 1)
            done(dve.memset(ones[:], 1.0))
            done(dve.memset(gpad[:], NEG))
            dve.wait_ge(iota_ld, 16)
            done(dve.tensor_copy(gpad[:, :, 0:NG], g.logits[:, :, 0:NG]))
            for t in range(TT):
                last = dve.max(gmx[:, t], gpad[:, t])
            done(last)
            for t in range(TT):
                last = dve.max_index(gix[:, t], gmx[:, t], gpad[:, t])
            done(last)
            done(dve.tensor_copy(gi[:], gix[:, :, 0]))
            done(dve.tensor_tensor(gex[:], g.logits[:, :, 0:NG], gmx[:, :, 0:1].to_broadcast([P, TT, NG]),
                                   ALU.subtract))
            dve.sem_inc(gexp, 1)
            done(dve.tensor_tensor(goh[:], iota[:, 0:NG].unsqueeze(1).to_broadcast([P, TT, NG]),
                                   gi[:].unsqueeze(2).to_broadcast([P, TT, NG]), ALU.is_equal))
            done(dve.tensor_tensor(em[:], g.logits[:, :, NG:].rearrange("p t (g e) -> p t g e", g=NG),
                                   goh[:].unsqueeze(3).to_broadcast([P, TT, NG, EPG]), ALU.mult))
            done(dve.tensor_reduce(es[:], em[:].rearrange("p t g e -> p t e g"), AX.X, ALU.add))
            for t in range(TT):
                last = dve.max(emx[:, t], es[:, t])
            done(last)
            for t in range(TT):
                last = dve.max_index(eix[:, t], emx[:, t], es[:, t])
            done(last)
            done(dve.tensor_tensor(tmp[:, 0], emx[:, :, 1], emx[:, :, 0], ALU.subtract))
            dve.sem_inc(eexp, 1)
            done(dve.tensor_copy(eid[:], eix[:, :, 0:2].rearrange("p t k -> p k t")))
            done(dve.scalar_tensor_tensor(eid[:], gi[:].unsqueeze(1).to_broadcast([P, 2, TT]), float(EPG), eid[:],
                                          op0=ALU.mult, op1=ALU.add))
            for k in range(2):
                last = dve.tensor_tensor(oh[:, k], iota[:, 0:NE].unsqueeze(1).to_broadcast([P, TT, NE]),
                                         over_e(eid[:, k]), ALU.is_equal)
            done(last)
            done(dve.tensor_tensor(both[:], oh[:, 0], oh[:, 1], ALU.add))
            done(dve.memset(both[TS:P, NT, :], 0.0))
            dve.sem_inc(rank_mm, 1)
            dve.wait_ge(gexp, 2)
            done(dve.tensor_reduce(pg[:, 0], gex[:], AX.X, ALU.add))
            dve.wait_ge(eexp, 2)
            done(dve.tensor_scalar(tmp[:, 2], tmp[:, 1], 1.0, None, ALU.add))
            done(dve.tensor_tensor(tmp[:, 3], pg[:, 0], tmp[:, 2], ALU.mult))
            done(dve.reciprocal(g.wt[:, 0], tmp[:, 3]))
            done(dve.tensor_tensor(g.wt[:, 1], g.wt[:, 0], tmp[:, 1], ALU.mult))
            done(dve.memset(pre[:, 0], 0.0))
            dve.wait_ge(rank_mm, 2)
            for t in range(TT):
                done(dve.tensor_tensor(pre[:, t + 1], pre[:, t], psC[:, t * NE:(t + 1) * NE], ALU.add))
            done(dve.tensor_scalar(cnt_i[:, 0], pre[:, TT], float(BLK - 1), None, ALU.add))
            done(dve.tensor_scalar(cnt_i[:, 1], cnt_i[:, 0], 7, None, ALU.arith_shift_right))
            done(dve.tensor_copy(cnt[:, 0], cnt_i[:, 1]))
            done(dve.tensor_tensor_scan(cnt[:, 1], ones[:, 0:NE], cnt[:, 0], 0.0, ALU.mult, ALU.add))
            done(dve.tensor_tensor(cnt[:, 2], cnt[:, 1], cnt[:, 0], ALU.subtract))
            done(dve.tensor_scalar(cnt[:, 3], cnt[:, 2], float(BLK), None, ALU.mult))
            done(dve.tensor_tensor(rank[:], pre[:, 0:TT], psR[:].rearrange("p (t e) -> p t e", e=NE), ALU.add))
            done(dve.tensor_tensor(rank[:], rank[:], cnt[:, 3].unsqueeze(1).to_broadcast([P, TT, NE]), ALU.add))
            done(dve.tensor_tensor(picked[:], oh[:], rank[:].unsqueeze(1).to_broadcast([P, 2, TT, NE]), ALU.mult))
            done(dve.tensor_reduce(dest_f[:], picked[:], AX.X, ALU.add))
            dve.tensor_copy(g.dest[:], dest_f[:]).then_inc(dest_done, 1)
            done(dve.tensor_tensor(cmp[:], cnt[0:1, 1].unsqueeze(1).to_broadcast([1, NBLK, NE]),
                                   iota[0:1].unsqueeze(2).to_broadcast([1, NBLK, NE]), ALU.is_le))
            done(dve.tensor_reduce(ctl_f[:, 0:NBLK], cmp[:], AX.X, ALU.add))
            done(dve.tensor_scalar(ctl_f[:, 0:NBLK], ctl_f[:, 0:NBLK], float(NE - 1), None, ALU.min))
            done(dve.tensor_scalar(ctl_f[:, NBLK:], cnt[0:1, 1, NE - 1:NE], 3.0, None, ALU.subtract))
            done(dve.tensor_copy(g.ctl[:], ctl_f[:]))


def expert_phase(nc, sem, g, A):
    with ExitStack() as c:
        def sb(name, shape, dt):
            return c.enter_context(nc.sbuf_tensor(name, shape, dt))

        GU = 2 * DE
        gu32 = sb("e_gu32", [P, 2, KC * GU], F32)
        d32 = sb("e_d32", [P, 2, 2 * D], F32)
        gu_h = sb("e_gu_h", [P, 2, KC, GU], F16)
        gu_l = sb("e_gu_l", [P, 2, KC, GU], F16)
        d_h = sb("e_d_h", [P, 2, 2, D], F16)
        d_l = sb("e_d_l", [P, 2, 2, D], F16)
        pairs = sb("e_pairs", [P, NBLK + 1], U32)
        idx = sb("e_idx", [P, 1], U32)
        idx_y = sb("e_idx_y", [P, 1], U32)
        xg = sb("e_xg", [P, D], F32)
        xT_h = sb("e_xT_h", [P, KC, P], F16)
        xT_l = sb("e_xT_l", [P, KC, P], F16)
        th = sb("e_th", [P, DE], F32)
        sg = sb("e_sg", [P, DE], F32)
        hid = sb("e_hid", [P, DE], F32)
        hT_h = sb("e_hT_h", [P, 2, P], F16)
        hT_l = sb("e_hT_l", [P, 2, P], F16)
        y_o = sb("e_y", [P, D], F32)
        psT = c.enter_context(nc.psum_tensor("e_psT", [P, KC, P], F32))
        psG = c.enter_context(nc.psum_tensor("e_psG", [P, 2, GU], F32))
        psH = c.enter_context(nc.psum_tensor("e_psH", [P, 2, P], F32))
        psY = c.enter_context(nc.psum_tensor("e_psY", [P, D], F32))
        gu_ld, d_ld, idx_ld, xg_ld, y_st = (sem("e_" + n) for n in ("gu_ld", "d_ld", "idx_ld", "xg_ld", "y_st"))
        gu_high, gu_low, d_high, d_low = (sem("e_" + n) for n in ("gu_high", "gu_low", "d_high", "d_low"))
        xT_done, xT_high, xT_low, gu_mm, th_done, sg_done, hid_done = (
            sem("e_" + n) for n in ("xT", "xT_high", "xT_low", "gu_mm", "th", "sg", "hid"))
        hT_done, hT_high, hT_low, y_mm, y_out = (sem("e_" + n) for n in ("hT", "hT_high", "hT_low", "y_mm", "y_out"))
        gather_go, scatter_go, idx_done, idx_y_done = (
            sem("e_" + n) for n in ("gather_go", "scatter_go", "idx", "idx_y"))
        block = c.enter_context(nc.Block())

        def slot(buf, n):
            if isinstance(n, int):
                return buf[:, n % 2]
            return buf[:, ds(n % 2, 1)].rearrange("p a n -> p (a n)")

        def slot3(buf, n):
            if isinstance(n, int):
                return buf[:, n % 2]
            return buf[:, ds(n % 2, 1)].rearrange("p a k n -> p (a k) n")

        halves = (slice(0, KC // 2), slice(KC // 2, KC))

        def chunks32(b):
            return slot(gu32, b).rearrange("p (k n) -> p k n", k=KC)

        def blocks(eng):
            return eng.value_load(g.ctl[0:1, NBLK:NBLK + 1], min_val=0, max_val=NBLK - 3)

        @block.sync
        def _(sp):
            more = blocks(sp)

            def load_gate_up(b):
                e = sp.value_load(g.ctl[0:1, ds(b, 1)], min_val=0, max_val=NE - 1)
                sp.wait_ge(gu_ld, 16 * b)
                sp.wait_ge(gu_low, b)
                sp.dma_start(slot(gu32, b), A["w_gu"][ds(e, 1)].rearrange("a p n -> (a p) n")).then_inc(gu_ld, 16)

            def load_down(b):
                e = sp.value_load(g.ctl[0:1, ds(b, 1)], min_val=0, max_val=NE - 1)
                sp.wait_ge(d_ld, 16 * b)
                sp.wait_ge(d_low, b)
                sp.dma_start(slot(d32, b), A["w_dn"][ds(e, 1)].rearrange("a p n -> (a p) n")).then_inc(d_ld, 16)

            e0 = sp.value_load(g.ctl[0:1, 0:1], min_val=0, max_val=NE - 1)
            sp.dma_start(gu32[:, 0], A["w_gu"][ds(e0, 1)].rearrange("a p n -> (a p) n")).then_inc(gu_ld, 16)
            with sp.Fori(0, more + 2) as b:
                load_gate_up(b + 1)
                load_down(b)
            load_down(more + 2)

        @block.gpsimd
        def _(pool):
            more = blocks(pool)

            def gather(b):
                pool.tensor_copy(idx[:], pairs[:, ds(b, 1)]).then_inc(idx_done, 1)
                pool.wait_ge(idx_done, b + 1)
                pool.wait_ge(xT_done, b)
                pool.sem_inc(gather_go, 1)
                pool.indirect_dma_start(out=xg[:], out_offset=None, in_=A["hn_dram"],
                                        in_offset=bass.IndirectOffsetOnAxis(ap=idx[:], axis=0)).then_inc(xg_ld, 16)

            def next_gather(b):
                pool.wait_ge(xg_ld, 16 * b)
                gather(b)

            def scatter(b):
                pool.wait_ge(y_st, 16 * b)
                pool.tensor_copy(idx_y[:], pairs[:, ds(b, 1)]).then_inc(idx_y_done, 1)
                pool.wait_ge(idx_y_done, b + 1)
                pool.wait_ge(y_out, b + 1)
                pool.sem_inc(scatter_go, 1)
                pool.indirect_dma_start(out=A["y_dram"],
                                        out_offset=bass.IndirectOffsetOnAxis(ap=idx_y[:], axis=0),
                                        in_=y_o[:], in_offset=None).then_inc(y_st, 16)

            pool.dma_start(pairs[:], A["pair_dram"].rearrange("(b p) a -> p (b a)", p=P),
                           allow_slow_non_contiguous=True).then_inc(idx_ld, 16)
            pool.wait_ge(idx_ld, 16)
            gather(0)
            next_gather(1)
            next_gather(2)
            with pool.Fori(0, more + 1) as b:
                next_gather(b + 3)
                scatter(b)
            scatter(more + 1)
            scatter(more + 2)
            pool.wait_ge(y_st, 16 * more + 48)
            pool.sem_inc(scatter_go, 1)

        @block.scalar
        def _(act):
            more = blocks(act)

            def cut(b, half, first=False):
                act.wait_ge(gu_ld, 16 * b + 16)
                if not first:
                    act.wait_ge(gu_mm, b - 1)
                act.activation(slot3(gu_h, b)[:, halves[half]], chunks32(b)[:, halves[half]], ACT.Copy,
                               scale=S_W).then_inc(gu_high, 1)

            def cut_down(b, first=False):
                act.wait_ge(d_ld, 16 * b + 16)
                if not first:
                    act.wait_ge(y_mm, b - 1)
                act.activation(slot3(d_h, b), slot(d32, b).rearrange("p (k n) -> p k n", k=2), ACT.Copy,
                               scale=S_W).then_inc(d_high, 1)

            def rows(b):
                act.wait_ge(xT_done, b + 1)
                act.wait_ge(gu_mm, b)
                act.activation(xT_h[:], psT[:], ACT.Copy, scale=S_X).then_inc(xT_high, 1)

            def gate(b):
                act.wait_ge(gu_mm, b + 1)
                act.wait_ge(sg_done, b)
                act.activation(th[:], slot(psG, b)[:, 0:DE], ACT.Tanh, scale=0.5 * UNSCALE).then_inc(th_done, 1)

            def result(b):
                act.wait_ge(y_mm, b + 1)
                act.wait_ge(y_st, 16 * b)
                act.activation(y_o[:], psY[:], ACT.Copy, scale=1.0 / (S_H * S_W)).then_inc(y_out, 1)

            def hidden(b):
                act.wait_ge(hT_done, b + 1)
                act.wait_ge(y_mm, b)
                act.activation(hT_h[:], psH[:], ACT.Copy, scale=0.5 * UNSCALE * UNSCALE * S_H).then_inc(hT_high, 1)

            def tail(b):
                gate(b)
                rows(b + 1)
                result(b - 1)

            for half in range(2):
                cut(0, half, True)
            cut_down(0, True)
            rows(0)
            for half in range(2):
                cut(1, half, True)
            gate(0)
            cut(2, 0)
            rows(1)
            cut(2, 1)
            cut_down(1, True)
            hidden(0)
            with act.Fori(1, more + 1) as b:
                gate(b)
                cut(b + 2, 0)
                rows(b + 1)
                cut(b + 2, 1)
                result(b - 1)
                cut_down(b + 1)
                hidden(b)
            tail(more + 1)
            cut_down(more + 2)
            hidden(more + 1)
            tail(more + 2)
            hidden(more + 2)
            result(more + 2)

        @block.vector
        def _(dve):
            more = blocks(dve)
            dve.sem_inc(gu_low, 1)
            dve.sem_inc(d_low, 1)

            def low(b, half):
                dve.wait_ge(gu_high, 2 * b + half + 1)
                cut = dve.scalar_tensor_tensor(slot3(gu_l, b)[:, halves[half]], chunks32(b)[:, halves[half]], S_W,
                                               slot3(gu_h, b)[:, halves[half]], op0=ALU.mult, op1=ALU.subtract)
                if half:
                    cut.then_inc(gu_low, 1)

            def low_down(b):
                dve.wait_ge(d_high, b + 1)
                dve.scalar_tensor_tensor(slot3(d_l, b), slot(d32, b).rearrange("p (k n) -> p k n", k=2), S_W,
                                         slot3(d_h, b), op0=ALU.mult, op1=ALU.subtract).then_inc(d_low, 1)

            def rows(b):
                dve.wait_ge(xT_high, b + 1)
                dve.scalar_tensor_tensor(xT_l[:], psT[:], S_X, xT_h[:], op0=ALU.mult,
                                         op1=ALU.subtract).then_inc(xT_low, 1)

            def gate(b):
                dve.wait_ge(th_done, b + 1)
                dve.scalar_tensor_tensor(sg[:], th[:], 1.0, slot(psG, b)[:, 0:DE], op0=ALU.add,
                                         op1=ALU.mult).then_inc(sg_done, 1)
                dve.wait_ge(sg_done, b + 1)
                dve.tensor_tensor(hid[:], sg[:], slot(psG, b)[:, DE:GU], ALU.mult).then_inc(hid_done, 1)

            def hidden(b):
                dve.wait_ge(hT_high, b + 1)
                dve.scalar_tensor_tensor(hT_l[:], psH[:], 0.5 * UNSCALE * UNSCALE * S_H, hT_h[:], op0=ALU.mult,
                                         op1=ALU.subtract).then_inc(hT_low, 1)

            for half in range(2):
                low(0, half)
            low_down(0)
            rows(0)
            for half in range(2):
                low(1, half)
            with dve.Fori(0, more + 1) as b:
                gate(b)
                low(b + 2, 0)
                rows(b + 1)
                low(b + 2, 1)
                low_down(b + 1)
                hidden(b)
            gate(more + 1)
            rows(more + 2)
            low_down(more + 2)
            hidden(more + 1)
            gate(more + 2)
            rows(more + 3)
            hidden(more + 2)

        @block.tensor
        def _(pe):
            more = blocks(pe)

            def turn(b):
                pe.wait_ge(xg_ld, 16 * b + 16)
                pe.wait_ge(xT_low, b)
                for k in range(KC):
                    last = pe.transpose(psT[:, k, :], xg[:, k * P:(k + 1) * P], g.ident[:])
                last.then_inc(xT_done, 1)

            def gate_up(b, first=False):
                pe.wait_ge(gu_low, b + 2)
                pe.wait_ge(xT_low, b + 1)
                if not first:
                    pe.wait_ge(hid_done, b - 1)
                for k in range(KC):
                    last = mm3(pe, slot(psG, b), (xT_h[:, k, :], xT_l[:, k, :]),
                               (slot3(gu_h, b)[:, k], slot3(gu_l, b)[:, k]), k == 0, k == KC - 1)
                last.then_inc(gu_mm, 1)

            def turn_hidden(b):
                pe.wait_ge(hid_done, b + 1)
                pe.wait_ge(hT_low, b)
                for k in range(2):
                    last = pe.transpose(psH[:, k, :], hid[:, k * P:(k + 1) * P], g.ident[:])
                last.then_inc(hT_done, 1)

            def down(b):
                pe.wait_ge(d_low, b + 2)
                pe.wait_ge(hT_low, b + 1)
                pe.wait_ge(y_out, b)
                for n in range(2):
                    cols = slice(n * 512, (n + 1) * 512)
                    for k in range(2):
                        last = mm3(pe, psY[:, cols], (hT_h[:, k, :], hT_l[:, k, :]),
                                   (slot3(d_h, b)[:, k, cols], slot3(d_l, b)[:, k, cols]), k == 0, k == 1)
                last.then_inc(y_mm, 1)

            turn(0)
            gate_up(0, True)
            turn(1)
            turn_hidden(0)
            with pe.Fori(1, more + 3) as b:
                gate_up(b)
                turn(b + 1)
                down(b - 1)
                turn_hidden(b)
            down(more + 2)


def combine_phase(nc, sem, g, A):
    with ExitStack() as c:
        rows = c.enter_context(nc.sbuf_tensor("f_rows", [P, TT, 2, D], F32))
        got, first, both, out_st = sem("f_got"), sem("f_first"), sem("f_both"), sem("f_out")
        block = c.enter_context(nc.Block())

        def height(t):
            return P if t < NT else TS

        @block.vector
        def _(dve):
            for t in range(TT):
                n = height(t)
                for k, s in enumerate((first, both)):
                    dve.wait_ge(got, 16 * (t + 1))
                    if k:
                        dve.wait_ge(first, t + 1)
                    dve.scalar_tensor_tensor(g.h[0:n, t, :], rows[0:n, t, k, :], g.wt[0:n, k, t:t + 1],
                                             g.h[0:n, t, :], op0=ALU.mult, op1=ALU.add).then_inc(s, 1)

        @block.sync
        def _(sp):
            pairs = A["y_dram"].rearrange("(k r) d -> r k d", k=2)
            for t in range(TT):
                sp.wait_ge(got, 16 * t)
                sp.dma_start(rows[0:height(t), t], pairs[t * P:t * P + height(t)]).then_inc(got, 16)
            for t in range(TT):
                n = height(t)
                sp.wait_ge(both, t + 1)
                sp.dma_start(A["y_all"][t * P:t * P + n, :], g.h[0:n, t, :]).then_inc(out_st, 16)
            sp.wait_ge(out_st, 16 * TT)


def program(nc, arrays, debug=None):
    A = dict(arrays)
    A["dist_dram"] = nc.dram_tensor("dist_dram", [COPIES * NH, RW], F32).ap()
    A["gates"] = nc.dram_tensor("gates", [2 * KC, P, TM], F32).ap()
    A["hn_dram"] = nc.dram_tensor("hn_dram", [2 * TP, D], F32).ap()
    A["pair_dram"] = nc.dram_tensor("pair_dram", [(NBLK + 1) * BLK, 1], U32).ap()
    A["y_dram"] = nc.dram_tensor("y_dram", [2 * TP, D], F32).ap()
    g = OnChip()
    with ExitStack() as c:
        def sb(name, shape, dt, ctx=c):
            return ctx.enter_context(nc.sbuf_tensor(name, shape, dt))

        held = []

        def sem(name):
            held.append(nc.alloc_semaphore(name=name))
            return held[-1]

        def phase_end():
            nc.clear_and_free_semaphores(list(held))
            held.clear()
            nc.all_engine_barrier()

        g.ident = sb("ident", [P, P], F32)
        g.neg_half = sb("neg_half", [P, NH + NKV], F32)
        big = g.big = sb("big", [P, KC * TP], F32)
        g.y = big[:, 0:KC * TM].rearrange("p (k n) -> p k n", k=KC)
        pair = big[:].bitcast(F16).rearrange("p (a k n) -> p a k n", a=2, k=KC)
        g.mT_h, g.mT_l = pair[:, 0], pair[:, 1]
        with ExitStack() as c1:
            g.xnT_h = sb("xnT_h", [P, KC, TP], F16, c1)
            g.xnT_l = sb("xnT_l", [P, KC, TP], F16, c1)
            g.oT_h = sb("oT_h", [P, KC, TP], F16, c1)
            g.oT_l = sb("oT_l", [P, KC, TP], F16, c1)
            with ExitStack() as c2:
                g.q_s = sb("q_s", [P, D], F32, c2)
                g.k_s = sb("k_s", [P, KVW], F32, c2)
                g.v_s = sb("v_s", [P, KVW], F32, c2)
                with ExitStack() as c3:
                    g.qkv = sb("qkv", [P, 2, QKVW], F32, c3)
                    g.w_qkv_l = sb("w_qkv_l", [P, KC, QKVW], F16, c3)
                    norm_phase(nc, sem, g, A)
                    attention_phase(nc, sem, g, A)
                sample_phase(nc, sem, g, A)
            phase_end()
            g.caT_h = sb("caT_h", [P, KC, TM], F16, c1)
            g.caT_l = sb("caT_l", [P, KC, TM], F16, c1)
            conv_phase(nc, sem, g, A)
            merge_phase(nc, sem, g, A)
            if debug:
                debug(nc, sem, g, A)
        g.h = sb("h", [P, TT, D], F32)
        g.logits = sb("logits", [P, TT, RT], F32)
        g.dest = sb("dest", [P, 2, TT], U32)
        g.wt = sb("wt", [P, 2, TT], F32)
        g.ctl = sb("ctl", [1, NBLK + 1], I32)
        out_phase(nc, sem, g, A)
        route_phase(nc, sem, g, A)
        phase_end()
        expert_phase(nc, sem, g, A)
        combine_phase(nc, sem, g, A)


def layout(x_prompt, x_sample, state_conv, cache_k, cache_v, norm_attn_g, w_in, q_norm_g, k_norm_g, rel_bias,
           attn_sinks, w_dw, b_dw, conv_ln_g, conv_ln_b, w_conv_out, b_conv_out, w_attn_out, w_out, norm_ffn_g,
           w_grp, b_grp, w_router, b_router, w_gate, w_up, w_down):
    f = np.float32
    x_all = np.zeros((TP, D), f)
    x_all[0:SEQ] = x_prompt.reshape(SEQ, D)
    x_all[SEQ:T] = x_sample.reshape(TS, D)

    def chunks(w):
        return w.reshape(KC, P, -1, P).transpose(2, 1, 0, 3).reshape(-1, P, KC * P)

    def by_channel(v):
        return v.reshape(KC, P).T

    bag = np.stack([chunks(w_in[:, c:c + D]) for c in (COL_B, COL_A, COL_GA)], 1)
    gate_b = chunks(w_in[:, COL_GB:COL_GB + D])
    merge = np.stack([chunks(w_conv_out), chunks(w_attn_out)], 1)
    gu = np.concatenate([w_gate, w_up], 2).reshape(NE, KC, P, 2 * DE).transpose(0, 2, 1, 3).reshape(NE, P, -1)
    dn = w_down.reshape(NE, 2, P, D).transpose(0, 2, 1, 3).reshape(NE, P, -1)
    dist = 2 * P - 1 - np.arange(RW)
    n = np.maximum(dist, 0)
    large = NB // 2 + (np.log(np.maximum(n, 1).astype(f) / f(NB // 2)) / f(np.log(128 / (NB // 2)))
                       * f(NB - NB // 2)).astype(np.int32)
    bucket = np.where(n < NB // 2, n, np.minimum(large, NB - 1))
    inside = (dist >= 0) & (dist < WIN)
    c_bucket = ((bucket[None, :] == np.arange(NB)[:, None]) & inside[None, :]).astype(f)
    c_mask = np.broadcast_to(np.where(inside, f(0), f(NEG)), (NH, RW))
    return {k: np.ascontiguousarray(v) for k, v in {
        "x_all": x_all, "norm_attn_g": norm_attn_g, "w_in": w_in, "gq2": np.concatenate([q_norm_g] * 2)[:, None],
        "k_norm_g": k_norm_g, "rel_bias": rel_bias, "attn_sinks": attn_sinks,
        "cache_k": cache_k.reshape(NSEQ, WIN, KVW), "cache_v": cache_v.reshape(NSEQ, WIN, KVW),
        "ckT": cache_k.transpose(3, 2, 0, 1).reshape(HD, NKV * NSEQ, WIN),
        "cvT": cache_v.transpose(1, 0, 2, 3).reshape(WIN, NSEQ, KVW),
        "stateT": state_conv.transpose(2, 0, 1), "tapsT": w_dw.T.reshape(KC, P, TAPS).transpose(1, 0, 2),
        "conv_vecs": np.stack([by_channel(b_dw), by_channel(conv_ln_g), by_channel(conv_ln_b)], 1),
        "b_conv_outT": by_channel(b_conv_out),
        "w_feat": np.concatenate([bag.reshape(-1, P, KC * P), gate_b, merge.reshape(-1, P, KC * P)]),
        "w_out": w_out, "norm_ffn_g": norm_ffn_g,
        "w_rt": np.concatenate([w_grp, w_router], 1).reshape(KC, P, RT).transpose(1, 0, 2),
        "b_rt": np.concatenate([b_grp, b_router]), "w_gu": gu, "w_dn": dn,
        "c_ident": np.eye(P, dtype=f), "c_bucket": c_bucket, "c_mask": c_mask,
        "c_iota": np.broadcast_to(np.arange(NBLK, dtype=f), (P, NBLK)),
        "c_upper": np.triu(np.ones((P, P), f), 1)}.items()}


OUTPUTS = {"y_all": (T, D), "sc_prompt": (D, HIST), "ck_prompt": (WIN, KVW), "cv_prompt": (WIN, KVW),
           "sc_sample": (D, NSEQ, HIST), "ck_sample": (NSEQ, WIN, KVW), "cv_sample": (NSEQ, WIN, KVW)}


def kernel(**inputs):
    import concourse.bacc as bacc
    from concourse.bass_utils import run_bass_kernel_spmd

    nc = bacc.Bacc("TRN2", target_bir_lowering=False, num_devices=1)
    arrays = layout(**{k: np.asarray(v) for k, v in inputs.items()})
    aps = {n: nc.dram_tensor(n, a.shape, mybir.dt.from_np(a.dtype), kind="ExternalInput").ap()
           for n, a in arrays.items()}
    aps.update({n: nc.dram_tensor(n, s, F32, kind="ExternalOutput").ap() for n, s in OUTPUTS.items()})
    program(nc, aps)
    r = run_bass_kernel_spmd(nc, [arrays], core_ids=[0]).results[0]
    y = r["y_all"]
    kv = (WIN, NKV, HD)
    return (y[0:SEQ].reshape(1, SEQ, D), y[SEQ:].reshape(NSEQ, DSEQ, D), r["sc_prompt"].T.reshape(1, HIST, D),
            r["ck_prompt"].reshape(1, *kv), r["cv_prompt"].reshape(1, *kv),
            r["sc_sample"].transpose(1, 2, 0), r["ck_sample"].reshape(NSEQ, *kv),
            r["cv_sample"].reshape(NSEQ, *kv))
```
